# Optimizing a Trainium2 kernel written in Bass

```python
import math
import jax, jax.numpy as jnp
from jax import lax
import numpy as np

D_MODEL = 1024
BATCH = 1
SEQ = 256
DEPTH = 1

PLE_DIM = 256
MIX_WIDTH = D_MODEL
ATTN_WIDTH = MIX_WIDTH // 2
HYENA_WIDTH = MIX_WIDTH - ATTN_WIDTH
DIFF_HEADS = 4
DIFF_HEAD_DIM = ATTN_WIDTH // (2 * DIFF_HEADS)
DIFF_V_DIM = 2 * DIFF_HEAD_DIM
HYENA_GROUPS = 8
SHORT_CONV = 3
FILTER_EMB = 33
FILTER_ORDER = 64
FILTER_INNER = 2
FAST_DECAY_PCT = 0.3
SLOW_DECAY_PCT = 1.5
DECAY_TARGET = 1e-2
ROPE_THETA = 10000.0
N_EXPERTS = 32
TOP_K = 4
D_FF = D_MODEL
SWIGLU_ALPHA = 1.702
SWIGLU_LIMIT = 7.0
EXPERT_BLOCK = 256
Q_BLOCK = 128
EPS = 1e-6
SUBLN_EPS = 1e-5
IN_PROJ_WIDTH = 3 * ATTN_WIDTH + 3 * HYENA_WIDTH

kernel_name = 'hymba_diffattn_hyena_moe_block'

def rms_norm(x, g, eps=EPS):
    xf = x.astype(jnp.float32)
    y = xf * lax.rsqrt(jnp.mean(xf * xf, axis=-1, keepdims=True) + eps)
    return (y * g.astype(jnp.float32)).astype(x.dtype)

def apply_rope(x):
    S, d = x.shape[1], x.shape[-1]
    pos = jnp.arange(S, dtype=jnp.float32)
    inv = ROPE_THETA ** (-jnp.arange(0, d, 2, dtype=jnp.float32) / d)
    ang = pos[:, None] * inv[None, :]
    cos = jnp.cos(ang)[None, :, None, None, :]
    sin = jnp.sin(ang)[None, :, None, None, :]
    xf = x.astype(jnp.float32)
    x1, x2 = xf[..., : d // 2], xf[..., d // 2:]
    return jnp.concatenate([x1 * cos - x2 * sin, x2 * cos + x1 * sin], axis=-1).astype(x.dtype)

def diff_attention(q, k, v, lam, lambda_init, g_subln):
    B, S, H, _, dh = q.shape
    dv = v.shape[-1]
    scale = dh ** -0.5
    nq = S // Q_BLOCK
    qb = jnp.moveaxis(q.reshape(B, nq, Q_BLOCK, H, 2, dh), 1, 0)

    def block(qi):
        s = jnp.einsum('bqhcd,bkhcd->bhcqk', qi, k, preferred_element_type=jnp.float32) * scale
        pr = jax.nn.softmax(s, axis=-1)
        a = pr[:, :, 0] - lam * pr[:, :, 1]
        return jnp.einsum('bhqk,bkhe->bqhe', a.astype(v.dtype), v)

    o = lax.map(block, qb)
    o = jnp.moveaxis(o, 0, 1).reshape(B, S, H, dv)
    o = rms_norm(o, g_subln, SUBLN_EPS) * (1.0 - lambda_init)
    return o.reshape(B, S, H * dv)

def short_conv(x, w, b):
    half = SHORT_CONV // 2
    S = x.shape[1]
    xp = jnp.pad(x, ((0, 0), (half, SHORT_CONV - 1 - half), (0, 0)))
    y = b
    for j in range(SHORT_CONV):
        y = y + xp[:, j:j + S] * w[j]
    return y

def hyena_filters(seq, w1, b1, w_inner, b_inner, freq, w_out):
    f32 = jnp.float32
    pos = jnp.arange(seq, dtype=f32)
    t = pos / (seq - 1)
    bands = (FILTER_EMB - 1) // 2
    f = jnp.linspace(1e-4, bands - 1, bands, dtype=f32)
    fw = ((2.0 * math.pi / seq) * pos)[:, None] * f[None, :]
    z = jnp.concatenate([t[:, None], jnp.cos(fw), -jnp.sin(fw)], axis=-1)
    h = jnp.sin(freq[0].astype(f32) * (z @ w1.astype(f32) + b1.astype(f32)))
    for j in range(FILTER_INNER):
        h = jnp.sin(freq[j + 1].astype(f32) * (h @ w_inner[j].astype(f32) + b_inner[j].astype(f32)))
    h = h @ w_out.astype(f32)
    max_decay = math.log(DECAY_TARGET) / FAST_DECAY_PCT
    min_decay = math.log(DECAY_TARGET) / SLOW_DECAY_PCT
    deltas = jnp.abs(jnp.linspace(min_decay, max_decay, HYENA_WIDTH, dtype=f32))
    decay = jnp.exp(-t[:, None] * deltas[None, :])
    return h[:, :HYENA_WIDTH] * decay, h[:, HYENA_WIDTH:] * decay

def bidir_long_conv(u, h_fwd, h_bwd, d_skip):
    B, L, C = u.shape
    n = 2 * L
    lag0 = h_fwd[:1] + h_bwd[:1]
    kern = jnp.concatenate([lag0, h_fwd[1:], jnp.zeros((1, C), jnp.float32), h_bwd[:0:-1]], axis=0)
    u_f = jnp.fft.rfft(u.astype(jnp.float32), n=n, axis=1)
    k_f = jnp.fft.rfft(kern, n=n, axis=0)
    y = jnp.fft.irfft(u_f * k_f[None], n=n, axis=1)[:, :L]
    return (y + u.astype(jnp.float32) * d_skip.astype(jnp.float32)).astype(u.dtype)

def moe_ffn(h, router_w, router_b, w_gate, b_gate, w_up, b_up, w_down, b_down):
    B, S, D = h.shape
    T = B * S
    tok = h.reshape(T, D)
    logits = (tok @ router_w + router_b).astype(jnp.float32)
    top_logit, top_e = lax.top_k(logits, TOP_K)
    top_w = jax.nn.softmax(top_logit, axis=-1)
    A = T * TOP_K
    flat_e = top_e.reshape(A)
    order = jnp.argsort(flat_e)
    sorted_e = flat_e[order]
    sorted_tok = (order // TOP_K).astype(jnp.int32)
    sorted_w = top_w.reshape(A)[order]
    counts = jnp.bincount(flat_e, length=N_EXPERTS)
    padded = (counts + EXPERT_BLOCK - 1) // EXPERT_BLOCK * EXPERT_BLOCK
    pad_end = jnp.cumsum(padded)
    pad_start = pad_end - padded
    start = jnp.cumsum(counts) - counts
    dest = pad_start[sorted_e] + jnp.arange(A) - start[sorted_e]
    n_blocks = -(-A // EXPERT_BLOCK) + N_EXPERTS
    P = n_blocks * EXPERT_BLOCK
    slot_tok = jnp.full((P,), T, jnp.int32).at[dest].set(sorted_tok)
    slot_w = jnp.zeros((P,), jnp.float32).at[dest].set(sorted_w)
    block_e = jnp.minimum(
        jnp.searchsorted(pad_end, jnp.arange(n_blocks) * EXPERT_BLOCK, side='right'), N_EXPERTS - 1)
    tok_pad = jnp.concatenate([tok, jnp.zeros((1, D), tok.dtype)], axis=0)

    def expert_block(args):
        e, idx = args
        xb = tok_pad[idx]
        g = jnp.minimum(xb @ w_gate[e] + b_gate[e], SWIGLU_LIMIT)
        u = jnp.clip(xb @ w_up[e] + b_up[e], -SWIGLU_LIMIT, SWIGLU_LIMIT)
        a = (u + 1.0) * (g * jax.nn.sigmoid(SWIGLU_ALPHA * g))
        return a @ w_down[e] + b_down[e]

    y = lax.map(expert_block, (block_e, slot_tok.reshape(n_blocks, EXPERT_BLOCK)))
    y = y.reshape(P, D) * slot_w[:, None].astype(y.dtype)
    out = jax.ops.segment_sum(y, slot_tok, num_segments=T + 1)[:T]
    return out.reshape(B, S, D)

def setup_inputs(seed: int = 0) -> dict:
    key = jax.random.key(seed)
    ks = iter(jax.random.split(key, 48))

    def nrm(shape, scale):
        return jax.random.normal(next(ks), shape, jnp.float32) * scale

    def gain(shape):
        return 1.0 + nrm(shape, 0.02)

    Dh = HYENA_WIDTH
    return {
        'x': nrm((BATCH, SEQ, D_MODEL), 1.0),
        'p': nrm((DEPTH, BATCH, SEQ, PLE_DIM), 1.0),
        'g_mix': gain((DEPTH, D_MODEL)),
        'w_in': nrm((DEPTH, D_MODEL, IN_PROJ_WIDTH), D_MODEL ** -0.5),
        'hyena_conv_w': nrm((DEPTH, SHORT_CONV, 3 * Dh), SHORT_CONV ** -0.5),
        'hyena_conv_b': nrm((DEPTH, 3 * Dh), 0.02),
        'flt_w1': nrm((DEPTH, FILTER_EMB, FILTER_ORDER), FILTER_EMB ** -0.5),
        'flt_b1': nrm((DEPTH, FILTER_ORDER), 0.02),
        'flt_w_inner': nrm((DEPTH, FILTER_INNER, FILTER_ORDER, FILTER_ORDER), FILTER_ORDER ** -0.5),
        'flt_b_inner': nrm((DEPTH, FILTER_INNER, FILTER_ORDER), 0.02),
        'flt_freq': gain((DEPTH, FILTER_INNER + 1, FILTER_ORDER)),
        'flt_w_out': nrm((DEPTH, FILTER_ORDER, 2 * Dh), FILTER_ORDER ** -0.5),
        'hyena_d': nrm((DEPTH, Dh), 1.0),
        'hyena_gn': gain((DEPTH, Dh)),
        'lambda_q1': nrm((DEPTH, DIFF_HEAD_DIM), 0.1),
        'lambda_k1': nrm((DEPTH, DIFF_HEAD_DIM), 0.1),
        'lambda_q2': nrm((DEPTH, DIFF_HEAD_DIM), 0.1),
        'lambda_k2': nrm((DEPTH, DIFF_HEAD_DIM), 0.1),
        'attn_subln': gain((DEPTH, DIFF_V_DIM)),
        'w_out': nrm((DEPTH, MIX_WIDTH, D_MODEL), MIX_WIDTH ** -0.5),
        'g_ffn': gain((DEPTH, D_MODEL)),
        'router_w': nrm((DEPTH, D_MODEL, N_EXPERTS), D_MODEL ** -0.5),
        'router_b': nrm((DEPTH, N_EXPERTS), 0.01),
        'w_gate': nrm((DEPTH, N_EXPERTS, D_MODEL, D_FF), D_MODEL ** -0.5),
        'b_gate': nrm((DEPTH, N_EXPERTS, D_FF), 0.02),
        'w_up': nrm((DEPTH, N_EXPERTS, D_MODEL, D_FF), D_MODEL ** -0.5),
        'b_up': nrm((DEPTH, N_EXPERTS, D_FF), 0.02),
        'w_down': nrm((DEPTH, N_EXPERTS, D_FF, D_MODEL), D_FF ** -0.5),
        'b_down': nrm((DEPTH, N_EXPERTS, D_MODEL), 0.02),
        'w_ple': nrm((DEPTH, PLE_DIM, D_MODEL), PLE_DIM ** -0.5),
        'g_ple': gain((DEPTH, D_MODEL)),
        'w_ple_gate': nrm((DEPTH, D_MODEL, D_MODEL), D_MODEL ** -0.5),
        'b_ple_gate': nrm((DEPTH, D_MODEL), 0.02),
        'g_final': gain((D_MODEL,)),
    }

def reference(x, p, g_mix, w_in, hyena_conv_w, hyena_conv_b, flt_w1, flt_b1, flt_w_inner,
              flt_b_inner, flt_freq, flt_w_out, hyena_d, hyena_gn, lambda_q1, lambda_k1,
              lambda_q2, lambda_k2, attn_subln, w_out, g_ffn, router_w, router_b, w_gate,
              b_gate, w_up, b_up, w_down, b_down, w_ple, g_ple, w_ple_gate, b_ple_gate, g_final):
    B, S, _ = x.shape
    H, dh, dv = DIFF_HEADS, DIFF_HEAD_DIM, DIFF_V_DIM
    h = x
    for i in range(DEPTH):
        a = rms_norm(h, g_mix[i])
        proj = a @ w_in[i]
        q = proj[..., :ATTN_WIDTH].reshape(B, S, H, 2, dh)
        k = proj[..., ATTN_WIDTH:2 * ATTN_WIDTH].reshape(B, S, H, 2, dh)
        v = proj[..., 2 * ATTN_WIDTH:3 * ATTN_WIDTH].reshape(B, S, H, dv)
        hy_in = proj[..., 3 * ATTN_WIDTH:]

        lambda_init = 0.8 - 0.6 * math.exp(-0.3 * i)
        f32 = jnp.float32
        lam = (jnp.exp(jnp.sum(lambda_q1[i].astype(f32) * lambda_k1[i].astype(f32)))
               - jnp.exp(jnp.sum(lambda_q2[i].astype(f32) * lambda_k2[i].astype(f32)))
               + lambda_init)
        attn_out = diff_attention(apply_rope(q), apply_rope(k), v, lam, lambda_init, attn_subln[i])

        hy = short_conv(hy_in, hyena_conv_w[i], hyena_conv_b[i])
        hv = hy[..., :HYENA_WIDTH]
        hx0 = hy[..., HYENA_WIDTH:2 * HYENA_WIDTH]
        hx1 = hy[..., 2 * HYENA_WIDTH:]
        h_fwd, h_bwd = hyena_filters(S, flt_w1[i], flt_b1[i], flt_w_inner[i], flt_b_inner[i],
                                     flt_freq[i], flt_w_out[i])
        z = bidir_long_conv(hv * hx1, h_fwd, h_bwd, hyena_d[i]) * hx0
        z = rms_norm(z.reshape(B, S, HYENA_GROUPS, HYENA_WIDTH // HYENA_GROUPS),
                     hyena_gn[i].reshape(HYENA_GROUPS, HYENA_WIDTH // HYENA_GROUPS))
        hyena_out = z.reshape(B, S, HYENA_WIDTH)

        mix = jnp.concatenate([attn_out, hyena_out], axis=-1) @ w_out[i]
        h = h + mix

        h = h + moe_ffn(rms_norm(h, g_ffn[i]), router_w[i], router_b[i], w_gate[i], b_gate[i],
                        w_up[i], b_up[i], w_down[i], b_down[i])

        e = rms_norm(p[i] @ w_ple[i], g_ple[i])
        gate = jax.nn.sigmoid(h @ w_ple_gate[i] + b_ple_gate[i])
        h = h + gate * e
    return rms_norm(h, g_final)


_drawn_inputs = setup_inputs


def setup_inputs(seed=0):
    import zlib

    import numpy as np

    out = dict(_drawn_inputs(seed))
    spreads = {}
    factors = {'lambda_q1': 11.791,
     'attn_subln': 7.714,
     'b_gate': 8.0,
     'b_up': 23.955,
     'b_down': 30.644,
     'g_ple': 72.691,
     'b_ple_gate': 22.989,
     'g_final': 22.742,
     'hyena_conv_b': 2.969,
     'flt_b1': 3.657,
     'flt_b_inner': 2.71,
     'flt_freq': 4.354,
     'hyena_gn': 4.551,
     'g_ffn': 3.579,
     'router_b': 5.176}
    for name, (base, spread) in spreads.items():
        noise = np.random.default_rng([zlib.crc32(name.encode()), seed]).standard_normal(out[name].shape)
        drawn = base * np.exp(spread * noise) if base else spread * noise
        out[name] = __import__('jax').numpy.asarray(drawn.astype(out[name].dtype))
    for name, factor in factors.items():
        out[name] = (out[name] * factor).astype(out[name].dtype)
    return out
```

```python
import math
from contextlib import ExitStack

import numpy as np

import concourse.bass as bass
from concourse import mybir

F32 = mybir.dt.float32
BF16 = mybir.dt.bfloat16
I32 = mybir.dt.int32
ALU = mybir.AluOpType
ACT = mybir.ActivationFunctionType
AX = mybir.AxisListType

P = 128
D = 1024
S = 256
TI = S // P
KD = D // P
HW = 512
H = 4
DH = 64
SCALE = DH ** -0.5
LAMBDA_INIT = 0.8 - 0.6 * math.exp(0.0)
NFFT = 2 * S
EMB = 33
FO = 64
NE = 32
TOPK = 4
ALPHA = 1.702
LIMIT = 7.0
PLE = 256
SLOTS = 64
NB = NE + (S * TOPK - NE) // SLOTS
NBT = NB + 2
CHUNKS = 12
PARTS = 3
SHARED = 23680
GROUPS = (0, 1, 2, 3, 5, 4)
FAR = 4096.0
ROUND = 12582912.0
TWO_PI = (6.28125, 0.0019350051879882812, 3.0199159819567e-07)
PI_BELOW = 3.1415925

COLS = {}
for _name, _n in (("gmix", KD), ("cw", 36), ("cb", 12), ("dskip", 4), ("gn", 4), ("subln", 1), ("b1", 1),
                  ("binner", 2), ("freq", 3), ("lq", 2), ("lk", 2), ("cf", TI), ("eps6", 1), ("eps5", 1),
                  ("first", 1), ("ident", P), ("rot", P), ("blk", P), ("tri", P), ("ones", P),
                  ("slot2", 2 * SLOTS), ("blkno", NBT), ("blk64", NBT), ("tri32i", NE)):
    COLS[_name] = (sum(n for _, n in COLS.values()), _n)
NCOLS = sum(n for _, n in COLS.values())

INPUTS = ["x", "cols", "rope", "dft", "decay", "zt", "w_in", "flt_w1", "flt_w_inner", "flt_w_out", "w_out",
          "g_ffn", "router_w", "router_b", "w_gate", "b_gate", "w_up", "b_up", "w_down", "b_down",
          "pt", "w_ple", "g_ple", "w_ple_gate", "b_ple_gate", "g_final"]


def build(nc, a, out):
    with ExitStack() as ctx:
        def sb(name, shape, dt=F32):
            return ctx.enter_context(nc.sbuf_tensor(name, shape, dt))

        def sem(name):
            return ctx.enter_context(nc.semaphore(name))

        ring = sb("ring", [P, 12, 2048])
        h = sb("h", [P, TI, D])
        cols = sb("cols", [P, NCOLS])
        small = sb("small", [P, 256])
        rw = sb("rw", [P, KD, NE])
        rb = sb("rb", [P, NE])
        shared = sb("shared", [P, SHARED])

        def col(name, i=0, n=1, p=P):
            at = COLS[name][0] + i
            return cols[0:p, at:at + n]

        def mat(name, p=P):
            at, n = COLS[name]
            return cols[0:p, at:at + n]

        used = {"f": 0, "m": 0}

        def part(phase, n, p=P):
            at = used[phase]
            used[phase] += n
            assert used[phase] <= SHARED, used
            return shared[0:p, at:at + n]

        aT = part("f", 2048).rearrange("p (k t) -> p k t", k=KD)
        mixT = aT
        xn = part("f", 2048).rearrange("p (i d) -> p i d", i=TI)
        qrope = xn[:, 0].rearrange("p (c t) -> p c t", c=H)
        krope = xn[:, 1].rearrange("p (c t) -> p c t", c=H)
        raw = part("f", 1024).rearrange("p (c t) -> p c t", c=H)
        v = part("f", 1024).rearrange("p (i n) -> p i n", i=TI)
        E = part("f", 2048).rearrange("p (s c i k) -> p s c i k", s=2, c=2, i=TI)
        diffT = part("f", 1024).rearrange("p (s j q) -> p s j q", s=2, j=TI)
        o = raw
        hv = part("f", 1024).rearrange("p (c t) -> p c t", c=4)
        hx1 = part("f", 1024).rearrange("p (c t) -> p c t", c=4)
        hx0 = part("f", 1024).rearrange("p (c t) -> p c t", c=4)
        utm = part("f", 1024).rearrange("p (i c) -> p i c", i=TI)
        Kre = part("f", 1024).rearrange("p (i c) -> p i c", i=TI)
        Kim = part("f", 1024).rearrange("p (i c) -> p i c", i=TI)
        K0 = part("f", 512)
        rope = K0.rearrange("p (c t) -> p c t", c=2)
        prod = part("f", 2048).rearrange("p (n c) -> p n c", n=4)
        Yre = part("f", 1024).rearrange("p (i c) -> p i c", i=TI)
        Yim = part("f", 1024).rearrange("p (i c) -> p i c", i=TI)
        ffwd = prod[:, 0:2]
        fbwd = prod[:, 2:4]
        fsum = Yre
        fdif = Yim
        decay = utm
        cosf = part("f", 512).rearrange("p (i f) -> p i f", i=TI)
        sinu = part("f", 512).rearrange("p (i f) -> p i f", i=TI)
        sink = part("f", 512).rearrange("p (i f) -> p i f", i=TI)
        sing = part("f", 512).rearrange("p (i f) -> p i f", i=TI)
        fargs = ffwd.rearrange("p n c -> p (n c)")[0:FO, 0:768].rearrange("p (n t) -> p n t", n=3)
        fh = fbwd.rearrange("p n c -> p (n c)")[0:FO, 0:768].rearrange("p (n t) -> p n t", n=3)
        wf1 = part("f", FO, EMB)
        zt = part("f", S, EMB)
        wfi = part("f", 2 * FO, FO).rearrange("p (j n) -> p j n", j=2)
        wfo = Kim.rearrange("p i c -> p (i c)")[0:FO]
        sqa = E.rearrange("p s c i k -> p (s c i k)")[:, 0:1024].rearrange("p (c t) -> p c t", c=H)
        rsa = E.rearrange("p s c i k -> p (s c i k)")[:, 1024:2048].rearrange("p (c t) -> p c t", c=H)
        z = hv
        sqh = utm.rearrange("p i c -> p (i c)").rearrange("p (c t) -> p c t", c=4)
        rsh = prod[:, 0:2].rearrange("p n c -> p (n c)").rearrange("p (c t) -> p c t", c=4)

        tokT = part("m", 2048).rearrange("p (k t) -> p k t", k=KD)
        hT = tokT
        tok = part("m", 2048).rearrange("p (i d) -> p i d", i=TI)
        e = part("m", 2048).rearrange("p (i d) -> p i d", i=TI)
        wpg = part("m", 8192).rearrange("p (k n) -> p k n", k=KD)
        wple = wpg[:, 0:2]
        pt = wpg[:, 2, 0:512].rearrange("p (k t) -> p k t", k=2)
        gple = wpg[:, 3]
        gffn = wpg[:, 4]
        bdn = wpg[0:NE, 5]
        squares = part("m", D)
        g, u = squares[:, 0:512], squares[:, 512:D]
        sg = part("m", 512)
        act = part("m", 512)
        actT = part("m", 512)
        y_selwT = part("m", 512 + S)
        y, selwT = y_selwT[:, 0:512], y_selwT[:, 512:512 + S]
        xg = part("m", 512)
        sel = part("m", SLOTS).bitcast(BF16).rearrange("p (i s) -> p i s", i=TI)
        selw = part("m", 4 * SLOTS).rearrange("p (i s) -> p i s", i=TI)
        tok3 = [t.bitcast(BF16).rearrange("p (i d) -> p i d", i=TI) for t in (
            part("m", D), part("m", D), tokT.rearrange("p k t -> p (k t)")[:, 0:D])]
        bias3 = part("m", D, PARTS * NE).bitcast(BF16)
        bias_in = wpg[0:PARTS * NE, 6:8].rearrange("p a n -> p (a n)")
        bple = part("m", D, 1)
        gfin = part("m", D)

        def tiny(at, n, p=P):
            return small[0:p, at:at + n]

        ssq, std, rstd = tiny(0, 2), tiny(2, 2), tiny(4, 2)
        lamp, lame, nlam = tiny(6, 2, FO), tiny(8, 2), tiny(10, 1)
        subl = tiny(11, 1)
        mx, nmx, rs = tiny(12, 8), tiny(20, 8), tiny(28, 8)
        rsi = tiny(36, 8)
        rt = sb("rt", [P, 640])

        def rts(at, n, p=P):
            return rt[0:p, at:at + n]

        lg = rts(0, 64).rearrange("p (i e) -> p i e", i=TI)
        m8 = rts(64, 16).rearrange("p (i e) -> p i e", i=TI)
        gt = rts(80, 64).rearrange("p (i e) -> p i e", i=TI)
        eq = rts(144, 64).rearrange("p (i e) -> p i e", i=TI)
        ceq = rts(208, 64).rearrange("p (i e) -> p i e", i=TI)
        ew = rts(272, 64).rearrange("p (i e) -> p i e", i=TI)
        need, nm1, wsum, winv = rts(336, 2), rts(338, 2), rts(340, 2), rts(342, 2)
        blocks_used = rts(344, 2, NE)
        starts = rts(346, 2, NE)
        ne_, nonempty = blocks_used[:, 0:1], blocks_used[:, 1:2]
        st_, before_ = starts[:, 0:1], starts[:, 1:2]
        en_, c1, load16 = rts(348, 1, NE), rts(349, 1, NE), rts(350, 1, NE)
        oh = rts(352, NBT, NE)
        ohs = rts(402, NBT, NE)
        oh3 = rts(550, (NBT + 1) // 2, PARTS * NE).bitcast(BF16)
        onehot = rts(576, SLOTS // 2, PARTS * NE).bitcast(BF16)
        posb = rts(452, 2 * NBT).rearrange("p (i b) -> p i b", i=TI)
        pwT = sb("pwT", [NE, 2, S])
        wb = sb("wb", [P, TI, NBT])
        table = sb("table", [1, NBT + NE], I32)
        TB, TE = 0, NBT

        ps = [ctx.enter_context(nc.psum_tensor(f"bank{n}", [P, 512], F32)) for n in range(8)]

        def half(n, c):
            return ps[n][:, 256 * c:256 * c + 256]

        d_x, d_cols, d_flt, d_rope, d_dft, d_dec, d_rw = (sem(n) for n in (
            "d_x", "d_cols", "d_flt", "d_rope", "d_dft", "d_dec", "d_rw"))
        d_win = [sem(f"d_win{n}") for n in range(6)]
        d_wout, d_ple, d_gffn, d_bdn, d_tail, d_wpg = (sem(n) for n in (
            "d_wout", "d_ple", "d_gffn", "d_bdn", "d_tail", "d_wpg"))
        d_bias = sem("d_bias")
        d_w = [sem(f"d_w{c}") for c in range(12)]
        names = ("V Y a aTe aTs aTt aTv accfree bias3 cnt conv dT dTs df dout en eraw ers essq estd ew ex f1 "
                 "fa fd fdif fin fo fs fsq fstd fsum g gate gm gsig gx gxs h2 h2T h2Ts hres hsq hstd kim "
                 "kims kr kre kres lam lame lamp lg lgt mix mixa mixh nm1 nmx ny nys o onehot pb pos pr proj "
                 "projs pv pwT pwTs qr rawk rawq rotk rotq row rsa rsh sT sTs sc scat sel sg sna snh split "
                 "sqa sqh ssq start std tT tTs tab tabr tabv tok tok3 u uT uc ui ur used uts vv wr xT xn ye "
                 "yi z").split()
        s = {n: sem("s_" + n) for n in names}

        block = ctx.enter_context(nc.Block())
        wslot = [ring[:, c].rearrange("p (j n) -> p j n", j=2) for c in range(12)]
        win = [ring[:, 2 * n:2 * n + 2].rearrange("p a n -> p (a n)").rearrange("p (k n) -> p k n", k=KD)
               for n in range(6)]
        wout = ring[:, 8:12].rearrange("p a n -> p (a n)").rearrange("p (k n) -> p k n", k=KD)

        def expert_rows(w, ex, c):
            return w[0, ex, 256 * c:256 * c + 256].rearrange("(j p) n -> p j n", p=P)

        def expert_rows_at(w, ex, c):
            return w[0, bass.ds(ex, 1), 256 * c:256 * c + 256].rearrange("a (j p) n -> p (a j) n", p=P)

        CH = []
        for c in range(4):
            CH += [(2 * c, "w_gate", c), (2 * c + 1, "w_up", c)]
        CH += [(8 + c, "w_down", c) for c in range(4)]

        @block.sync
        def _(sp):
            sp.dma_start(h[:], a["x"][0].rearrange("(i p) d -> p i d", p=P)).then_inc(d_x, 16)
            sp.dma_start(cols[:], a["cols"]).then_inc(d_cols, 16)
            for n in range(2):
                sp.dma_start(win[n], a["w_in"][0, :, 512 * GROUPS[n]:512 * GROUPS[n] + 512].rearrange("(k p) n -> p k n", p=P)
                             ).then_inc(d_win[n], 16)
            sp.dma_start(rope, a["rope"]).then_inc(d_rope, 16)
            for n in range(2, 6):
                sp.dma_start(win[n], a["w_in"][0, :, 512 * GROUPS[n]:512 * GROUPS[n] + 512].rearrange("(k p) n -> p k n", p=P)
                             ).then_inc(d_win[n], 16)
            for slot, w, c in CH[:8]:
                sp.wait_ge(s["proj"], 2 * (slot // 2) + 2)
                sp.dma_start(wslot[slot], expert_rows(a[w], 0, c)).then_inc(d_w[slot], 16)
                if slot == 3:
                    sp.dma_start(rw[:], a["router_w"][0].rearrange("(k p) n -> p k n", p=P)).then_inc(d_rw, 16)
                    sp.dma_start(rb[:], a["router_b"][0:1, :].to_broadcast([P, NE])).then_inc(d_rw, 16)
            sp.wait_ge(s["proj"], 12)
            sp.dma_start(wout, a["w_out"][0].rearrange("(k p) n -> p k n", p=P)).then_inc(d_wout, 16)
            sp.wait_ge(s["mix"], 4)
            sp.dma_start(gffn, a["g_ffn"][0:1, :].to_broadcast([P, D])).then_inc(d_gffn, 16)
            for n in range(PARTS):
                rows = bias_in[NE * n:NE * n + NE]
                sp.dma_start(rows[:, 0:D], a["b_gate"][0]).then_inc(d_bias, 16)
                sp.dma_start(rows[:, D:2 * D], a["b_up"][0]).then_inc(d_bias, 16)
            sp.dma_start(wple, a["w_ple"][0].rearrange("(k p) n -> p k n", p=P)).then_inc(d_ple, 16)
            sp.dma_start(pt, a["pt"].rearrange("(k p) n -> p k n", p=P)).then_inc(d_ple, 16)
            sp.dma_start(gple, a["g_ple"][0:1, :].to_broadcast([P, D])).then_inc(d_ple, 16)
            sp.dma_start(bdn, a["b_down"][0]).then_inc(d_bdn, 16)
            for slot, w, c in CH[8:]:
                sp.dma_start(wslot[slot], expert_rows(a[w], 0, c)).then_inc(d_w[slot], 16)
            sp.dma_start(bple, a["b_ple_gate"][0:1, :]).then_inc(d_tail, 16)
            sp.dma_start(gfin, a["g_final"].rearrange("(a n) -> a n", a=1).to_broadcast([P, D])).then_inc(d_tail, 16)
            sp.wait_ge(s["tabr"], 2)
            with sp.Fori(0, NE - 1) as ex:
                before = sp.value_load(table[0:1, bass.ds(ex + TE, 1)], min_val=0, max_val=CHUNKS * NB)
                after = sp.value_load(table[0:1, bass.ds(ex + (TE + 1), 1)], min_val=0, max_val=CHUNKS * NB)
                with sp.If(before + 1 <= after):
                    nxt = ex + 1
                    for n, (slot, w, c) in enumerate(CH):
                        sp.wait_ge(s["used"], before + (n + 1))
                        sp.dma_start(wslot[slot], expert_rows_at(a[w], nxt, c)).then_inc(d_w[slot], 16)
            sp.wait_ge(s["en"], 2)
            sp.wait_ge(s["accfree"], 1)
            sp.dma_start(wpg, a["w_ple_gate"][0].rearrange("(k p) n -> p k n", p=P)).then_inc(d_wpg, 16)
            for i in range(TI):
                sp.wait_ge(s["fin"], i + 1)
                sp.dma_start(out[0, P * i:P * i + P, :], tok[:, i]).then_inc(s["dout"], 16)
            sp.wait_ge(s["dout"], 16 * TI)

        @block.gpsimd
        def _(pool):
            pool.wait_ge(s["fd"], 4)
            pool.tensor_tensor(fsum, ffwd, fbwd, ALU.add).then_inc(s["fsum"], 1)
            pool.tensor_tensor(fdif, ffwd, fbwd, ALU.subtract).then_inc(s["fdif"], 1)
            for f in range(TI):
                pool.wait_ge(s["pr"], 4 * f + 4)
                if f == 0:
                    pool.wait_ge(s["ny"], 1)
                pool.tensor_tensor(Yre[:, f], prod[:, 0], prod[:, 1], ALU.subtract).then_inc(s["Y"], 1)
                pool.tensor_tensor(Yim[:, f], prod[:, 2], prod[:, 3], ALU.add).then_inc(s["Y"], 1)
            pool.wait_ge(s["mix"], 4)
            pool.memset(y_selwT, 0.0).then_inc(s["ye"], CHUNKS)
            split = [0]

            def then(ins):
                split[0] += 1
                ins.then_inc(s["split"], 1)
                pool.wait_ge(s["split"], split[0])

            pool.wait_ge(s["tok"], 2)
            pool.wait_ge(s["tT"], 4)
            then(pool.tensor_copy(tok3[0], tok))
            then(pool.tensor_tensor(tok, tok, tok3[0], ALU.subtract))
            then(pool.tensor_copy(tok3[1], tok))
            pool.wait_ge(s["lgt"], 1)
            pool.tensor_tensor(tok3[2], tok, tok3[1], ALU.subtract).then_inc(s["tok3"], 1)
            pool.wait_ge(d_bias, 16 * 2 * PARTS)
            for n in (3, 2, 1):
                rows = slice(0, NE * n)
                m = pool.tensor_copy(bias3[rows], bias_in[rows])
                if n > 1:
                    then(m)
                    less = slice(0, NE * (n - 1))
                    then(pool.tensor_tensor(bias_in[less], bias_in[less], bias3[less], ALU.subtract))
                else:
                    m.then_inc(s["bias3"], 1)

        @block.scalar
        def _(sc):
            sc.dma_start(zt, a["zt"]).then_inc(d_flt, 16)
            sc.dma_start(wf1, a["flt_w1"][0]).then_inc(d_flt, 16)
            sc.dma_start(wfi, a["flt_w_inner"][0].rearrange("j p n -> p j n")).then_inc(d_flt, 16)
            sc.dma_start(wfo, a["flt_w_out"][0]).then_inc(d_flt, 16)
            sc.dma_start(decay, a["decay"].rearrange("(i p) n -> p i n", p=P)).then_inc(d_dec, 16)
            for n, t in enumerate((cosf, sinu, sink, sing)):
                sc.dma_start(t, a["dft"][n].rearrange("(i p) f -> p i f", p=P)).then_inc(d_dft, 16)

            def sin_layer(n):
                sc.wait_ge(s["fa"], n + 1)
                sc.activation(fh[:, n], fargs[:, 0], ACT.Sin).then_inc(s["fs"], 1)

            sc.wait_ge(d_x, 16)
            sc.wait_ge(d_cols, 16)
            for i in range(TI):
                sc.activation(xn[:, i], h[:, i], ACT.Square, accum_out=ssq[:, i:i + 1]).then_inc(s["ssq"], 1)
            sc.wait_ge(s["ssq"], 2)
            sc.activation(std, ssq, ACT.Sqrt, bias=col("eps6"), scale=1.0 / D).then_inc(s["std"], 1)
            sin_layer(0)
            for k in (2, 3, 6, 7):
                sc.wait_ge(s["xT"], k // 2 + 1)
                sc.activation(aT[:, k], half(k // 2, k % 2), ACT.Copy, scale=col("gmix", k)).then_inc(s["aTs"], 1)

            sin_layer(1)
            for n, name in ((0, "rawq"), (1, "rawk")):
                if n:
                    sc.wait_ge(s["rotq"], 1)
                    sc.wait_ge(s["qr"], 1)
                for b in range(2):
                    sc.wait_ge(s["proj"], 2 * n + b + 1)
                    sc.copy(raw[:, 2 * b:2 * b + 2].rearrange("p c t -> p (c t)"), ps[6 + b][:]).then_inc(s[name], 1)
                if n == 0:
                    sin_layer(2)
            for i in range(TI):
                sc.wait_ge(s["proj"], 5 + i)
                sc.copy(v[:, i], ps[6 + i][:]).then_inc(s["vv"], 1)

            def conv_first(n):
                dst = (hv, hx1, hx0)[n // 2]
                sc.wait_ge(s["proj"], 7 + n)
                for c in range(2):
                    ct = 4 * (GROUPS[3 + n // 2] - 3) + 2 * (n % 2) + c
                    sc.activation(dst[:, ct % 4], half(6 + n % 2, c), ACT.Identity, bias=col("cb", ct),
                                  scale=col("cw", 12 + ct)).then_inc(s["projs"], 1)

            def soft(hd):
                sl = hd % 2
                sc.wait_ge(s["nmx"], hd + 1)
                if hd >= 2:
                    sc.wait_ge(s["dT"], hd - 1)
                for c in range(2):
                    for i in range(TI):
                        at = 4 * sl + 2 * c + i
                        sc.activation(E[:, sl, c, i], half(2 * sl + c, i), ACT.Exp, bias=nmx[:, at:at + 1],
                                      scale=SCALE, accum_out=rs[:, at:at + 1]).then_inc(s["ex"], 1)

            def diff_turned(hd):
                sc.wait_ge(s["dT"], hd + 1)
                sc.copy(diffT[:, hd % 2].rearrange("p j q -> p (j q)"), ps[2 * (hd % 2)][:]).then_inc(s["dTs"], 1)

            def head_out(hd):
                sc.wait_ge(s["pv"], hd + 1)
                sc.copy(o[:, hd], half(2 * (hd % 2) + 1, 0)).then_inc(s["o"], 1)

            sc.wait_ge(s["lamp"], 1)
            sc.activation(lame, ps[5][:, 256:258], ACT.Exp).then_inc(s["lame"], 1)
            conv_first(0)
            soft(0)
            conv_first(1)
            soft(1)
            for f in range(TI):
                sc.wait_ge(s["kre"], f + 1)
                sc.activation(Kre[:, f], ps[4 + f][:], ACT.Copy, scale=col("cf", f)).then_inc(s["kres"], 1)
                if f == 0:
                    sc.activation(K0, ps[4][:], ACT.Copy, scale=col("cf", 0)).then_inc(s["kres"], 1)
            conv_first(2)
            diff_turned(0)
            for f in range(TI):
                sc.wait_ge(s["kim"], f + 1)
                sc.activation(Kim[:, f], ps[4 + f][:], ACT.Copy, scale=col("cf", f)).then_inc(s["kims"], 1)
            diff_turned(1)
            head_out(0)
            conv_first(3)
            sc.wait_ge(s["ny"], 1)
            sc.wait_ge(s["kres"], 3)
            sc.activation(K0[0:1, :], ps[4][0:1, :], ACT.Copy, scale=col("cf", 0, 1, 1)).then_inc(s["nys"], 1)
            head_out(1)
            soft(2)
            for i in range(TI):
                sc.wait_ge(s["uT"], i + 1)
                sc.copy(utm[:, i], ps[4 + i][:]).then_inc(s["uts"], 1)
            conv_first(4)
            soft(3)
            conv_first(5)
            diff_turned(2)
            diff_turned(3)
            head_out(2)
            head_out(3)
            sc.wait_ge(s["o"], 4)
            sc.wait_ge(s["dT"], 4)
            sc.activation(sqa, o, ACT.Square).then_inc(s["sqa"], 1)
            for n in range(2):
                sc.wait_ge(s["sna"], n + 1)
                sc.activation(rsa[:, 2 * n:2 * n + 2].rearrange("p c t -> p (c t)"), ps[2 * n][:], ACT.Sqrt,
                              bias=col("eps5"), scale=1.0 / P).then_inc(s["rsa"], 1)
            for c in range(4):
                sc.wait_ge(s["z"], c + 1)
                sc.activation(sqh[:, c], z[:, c], ACT.Square).then_inc(s["sqh"], 1)
            for n in range(2):
                sc.wait_ge(s["snh"], n + 1)
                sc.activation(rsh[:, 2 * n:2 * n + 2].rearrange("p c t -> p (c t)"), ps[4 + n][:], ACT.Sqrt,
                              bias=col("eps6"), scale=1.0 / 64).then_inc(s["rsh"], 1)

            for i in range(TI):
                sc.wait_ge(s["hres"], 2 * i + 2)
                sc.activation(tok[:, i], h[:, i], ACT.Square, accum_out=ssq[:, i:i + 1]).then_inc(s["hsq"], 1)
                sc.wait_ge(s["hsq"], i + 1)
                sc.activation(std[:, i:i + 1], ssq[:, i:i + 1], ACT.Sqrt, bias=col("eps6"), scale=1.0 / D
                              ).then_inc(s["hstd"], 1)
            for n in range(4):
                sc.wait_ge(s["tT"], n + 1)
                sc.copy(tokT[:, 2 * n:2 * n + 2].rearrange("p k t -> p (k t)"), ps[(1, 3, 4, 5)[n]][:]
                        ).then_inc(s["tTs"], 1)
            sc.wait_ge(s["nm1"], 2)
            for i in range(TI):
                sc.activation(ew[:, i], lg[:, i], ACT.Exp, bias=nm1[:, i:i + 1]).then_inc(s["ew"], 1)
            sc.wait_ge(s["pwT"], 2)
            sc.copy(pwT[:, 0], ps[4][0:NE, 0:S]).then_inc(s["pwTs"], 1)
            sc.copy(pwT[:, 1], ps[5][0:NE, 0:S]).then_inc(s["pwTs"], 1)
            for n in range(4):
                sc.wait_ge(s["eraw"], n + 1)
                sc.copy(e[:, n // 2, 512 * (n % 2):512 * (n % 2) + 512], ps[n][:]).then_inc(s["ers"], 1)
            sc.wait_ge(s["gx"], 1)
            sc.copy(xg, ps[6][:]).then_inc(s["gxs"], 1)
            sc.wait_ge(s["ers"], 4)
            for i in range(TI):
                sc.activation(squares, e[:, i], ACT.Square, accum_out=ssq[:, i:i + 1]).then_inc(s["essq"], 1)
                sc.wait_ge(s["essq"], i + 1)
            sc.activation(std, ssq, ACT.Sqrt, bias=col("eps6"), scale=1.0 / D).then_inc(s["estd"], 1)

            sc.wait_ge(s["tabr"], 2)
            blocks = sc.value_load(table[0:1, TE + NE - 1:TE + NE], min_val=0, max_val=CHUNKS * NB)
            with sc.Fori(0, NB) as b:
                with sc.If(b * CHUNKS <= blocks):
                    sc.wait_ge(s["g"], b + 1)
                    sc.activation(sg, g, ACT.Sigmoid, scale=ALPHA).then_inc(s["sg"], 1)
                    sc.wait_ge(s["sT"], b + 1)
                    sc.copy(selwT, ps[4][:, 0:S]).then_inc(s["sTs"], 1)
                    sc.wait_ge(s["aTt"], b + 1)
                    sc.copy(actT, ps[5][:]).then_inc(s["aTe"], 1)
                    sc.wait_ge(s["gx"], b + 2)
                    sc.copy(xg, ps[6][:]).then_inc(s["gxs"], 1)
                    sc.wait_ge(s["used"], b * CHUNKS + CHUNKS)
                    sc.copy(y, ps[7][:]).then_inc(s["ye"], CHUNKS)

            for n in range(4):
                sc.wait_ge(s["h2T"], n + 1)
                sc.copy(hT[:, 2 * n:2 * n + 2].rearrange("p k t -> p (k t)"), ps[4 + n][:]).then_inc(s["h2Ts"], 1)
            for n in range(4):
                i, hh = n // 2, n % 2
                sc.wait_ge(s["gate"], n + 1)
                sc.activation(tok[:, i, 512 * hh:512 * hh + 512], ps[n][:], ACT.Sigmoid).then_inc(s["gsig"], 1)
                if hh:
                    sc.wait_ge(s["gm"], 2 * i + 2)
                    sc.activation(tok[:, i], h[:, i], ACT.Square, accum_out=ssq[:, i:i + 1]).then_inc(s["fsq"], 1)
                    sc.wait_ge(s["fsq"], i + 1)
                    sc.activation(std[:, i:i + 1], ssq[:, i:i + 1], ACT.Sqrt, bias=col("eps6"), scale=1.0 / D
                                  ).then_inc(s["fstd"], 1)

        @block.tensor
        def _(pe):
            ident, ones = mat("ident"), mat("ones")

            def flt_layer(n):
                if n == 0:
                    pe.wait_ge(d_flt, 64)
                    pe.wait_ge(d_cols, 16)
                    pe.matmul(ps[5][0:FO, 0:S], wf1, zt, start=True, stop=True).then_inc(s["f1"], 1)
                else:
                    pe.wait_ge(s["fs"], n)
                    pe.matmul(ps[5][0:FO, 0:S], wfi[:, n - 1], fh[:, n - 1], start=True, stop=True
                              ).then_inc(s["f1"], 1)

            def project(n):
                grp, b = n // 2, n % 2
                if b == 0:
                    pe.wait_ge(d_win[grp], 16)
                if n in (2, 3):
                    pe.wait_ge(s["rawq"], b + 1)
                elif n in (4, 5):
                    pe.wait_ge(s["rawk"], b + 1)
                elif n in (6, 7):
                    pe.wait_ge(s["vv"], b + 1)
                elif n >= 8:
                    pe.wait_ge(s["conv"], 2 * (n - 8) + 2)
                if grp == 2:
                    for k in range(KD):
                        m = pe.matmul(ps[6 + b][:], aT[:, k, P * b:P * b + P], win[grp][:, k],
                                      start=k == 0, stop=k == KD - 1)
                else:
                    for c in range(2):
                        for k in range(KD):
                            at = P * (2 * b + c)
                            m = pe.matmul(half(6 + b, c), win[grp][:, k, at:at + P], aT[:, k],
                                          start=k == 0, stop=k == KD - 1)
                m.then_inc(s["proj"], 1)

            def rotate(name, done, b0):
                pe.wait_ge(s[name], 2)
                for c in range(2):
                    m = pe.matmul(ps[b0 + c][:], mat("rot"), raw[:, 2 * c:2 * c + 2].rearrange("p c t -> p (c t)"),
                                  start=True, stop=True)
                m.then_inc(s[done], 1)

            def flt_out(side):
                pe.wait_ge(s["fs"], 3)
                for i in range(TI):
                    if side:
                        pe.wait_ge(s["fd"], i + 1)
                    pe.matmul(ps[4 + i][:], fh[:, 2, P * i:P * i + P], wfo[:, HW * side:HW * side + HW],
                              start=True, stop=True).then_inc(s["fo"], 1)

            def scores(hd):
                sl = hd % 2
                for i in range(TI):
                    for c in range(2):
                        r = slice(DH * c, DH * c + DH)
                        m = pe.matmul(half(2 * sl + c, i), qrope[r, hd, P * i:P * i + P], krope[r, hd],
                                      start=True, stop=True)
                m.then_inc(s["sc"], 1)

            def turn_diff(hd):
                sl = hd % 2
                pe.wait_ge(s["df"], hd + 1)
                for j in range(TI):
                    for i in range(TI):
                        m = pe.transpose(ps[2 * sl][:, 256 * j + P * i:256 * j + P * i + P],
                                         E[:, sl, 0, i, P * j:P * j + P], ident)
                m.then_inc(s["dT"], 1)

            def apply_v(hd):
                sl = hd % 2
                pe.wait_ge(s["dTs"], hd + 1)
                for j in range(TI):
                    m = pe.matmul(half(2 * sl + 1, 0), v[:, j, P * hd:P * hd + P], diffT[:, sl, j],
                                  start=j == 0, stop=j == 1)
                m.then_inc(s["pv"], 1)

            def spectrum(banks, mat_, data, name):
                for f in range(TI):
                    for i in range(TI):
                        m = pe.matmul(ps[banks[f]][:], mat_[:, i, P * f:P * f + P], data[:, i],
                                      start=i == 0, stop=i == 1)
                    m.then_inc(s[name], 1)

            flt_layer(0)
            for n in range(4):
                for k in (2 * n, 2 * n + 1):
                    for i in range(TI):
                        pe.wait_ge(s["xn"], i + 1)
                        m = pe.transpose(ps[n][:, 256 * (k % 2) + P * i:256 * (k % 2) + P * i + P],
                                         xn[:, i, P * k:P * k + P], ident)
                m.then_inc(s["xT"], 1)
            pe.wait_ge(s["aTv"], 4)
            pe.wait_ge(s["aTs"], 4)
            project(0)
            flt_layer(1)
            project(1)
            project(2)
            rotate("rawq", "rotq", 0)
            flt_layer(2)
            project(3)
            project(4)
            rotate("rawk", "rotk", 2)
            pe.wait_ge(s["lam"], 1)
            pe.wait_ge(s["fs"], 3)
            pe.matmul(ps[5][:, 256:258], mat("ones", FO), lamp, start=True, stop=True).then_inc(s["lamp"], 1)
            project(5)
            pe.wait_ge(s["lame"], 1)
            flt_out(0)
            project(6)
            pe.wait_ge(s["kr"], 1)
            scores(0)
            flt_out(1)
            project(7)
            scores(1)
            pe.wait_ge(d_dft, 64)
            pe.wait_ge(s["fd"], 4)
            pe.wait_ge(s["fsum"], 1)
            spectrum((4, 5), cosf, fsum, "kre")
            project(8)
            turn_diff(0)
            pe.wait_ge(s["fdif"], 1)
            pe.wait_ge(s["kres"], 3)
            spectrum((4, 5), sink, fdif, "kim")
            apply_v(0)
            turn_diff(1)
            project(9)
            apply_v(1)
            pe.wait_ge(s["kims"], 2)
            for i in range(TI):
                m = pe.matmul(ps[4][0:1, :], sinu[:, i, 0:1], fsum[:, i], start=i == 0, stop=i == 1)
            m.then_inc(s["ny"], 1)
            pe.wait_ge(s["o"], 1)
            scores(2)
            project(10)
            pe.wait_ge(s["u"], 4)
            pe.wait_ge(s["nys"], 1)
            for i in range(TI):
                for c in range(4):
                    m = pe.transpose(ps[4 + i][:, P * c:P * c + P], hv[:, c, P * i:P * i + P], ident)
                m.then_inc(s["uT"], 1)
            pe.wait_ge(s["o"], 2)
            scores(3)
            project(11)
            pe.wait_ge(s["uts"], 2)
            spectrum((4, 5), cosf, utm, "ur")
            pe.wait_ge(s["conv"], 12)
            spectrum((6, 7), sinu, utm, "ui")
            turn_diff(2)
            turn_diff(3)
            apply_v(2)
            apply_v(3)
            pe.wait_ge(s["sqa"], 1)
            for n in range(2):
                pe.matmul(ps[2 * n][:], ones, sqa[:, 2 * n:2 * n + 2].rearrange("p c t -> p (c t)"),
                          start=True, stop=True).then_inc(s["sna"], 1)
            pe.wait_ge(s["Y"], 4)
            for c in range(4):
                terms = [(Yre, cosf, 0), (Yre, cosf, 1), (Yim, sing, 0), (Yim, sing, 1)]
                for n, (yy, w, f) in enumerate(terms):
                    m = pe.matmul(half(1 + 2 * (c // 2), c % 2), yy[:, f, P * c:P * c + P], w[:, f],
                                  start=n == 0, stop=n == 3)
                m.then_inc(s["yi"], 1)
            for n in range(2):
                pe.wait_ge(s["sqh"], 2 * n + 2)
                pe.wait_ge(s["pr"], 8)
                pe.matmul(ps[4 + n][:], mat("blk"), sqh[:, 2 * n:2 * n + 2].rearrange("p c t -> p (c t)"),
                          start=True, stop=True).then_inc(s["snh"], 1)

            pe.wait_ge(d_wout, 16)
            pe.wait_ge(s["mixa"], 4)
            banks = (0, 2, 6, 7)
            for n, bk in enumerate(banks):
                for k in range(4):
                    pe.matmul(ps[bk][:], mixT[:, k, P * (n // 2):P * (n // 2) + P],
                              wout[:, k, 512 * (n % 2):512 * (n % 2) + 512], start=k == 0, stop=False)
            pe.wait_ge(s["mixh"], 4)
            for n, bk in enumerate(banks):
                for k in range(4, KD):
                    m = pe.matmul(ps[bk][:], mixT[:, k, P * (n // 2):P * (n // 2) + P],
                                  wout[:, k, 512 * (n % 2):512 * (n % 2) + 512], start=False, stop=k == KD - 1)
                m.then_inc(s["mix"], 1)

            for n, bk in enumerate((1, 3, 4, 5)):
                for k in (2 * n, 2 * n + 1):
                    for i in range(TI):
                        pe.wait_ge(s["tok"], i + 1)
                        m = pe.transpose(ps[bk][:, 256 * (k % 2) + P * i:256 * (k % 2) + P * i + P],
                                         tok[:, i, P * k:P * k + P], ident)
                m.then_inc(s["tT"], 1)
            pe.wait_ge(d_rw, 32)
            pe.wait_ge(s["tTs"], 4)
            for i in range(TI):
                for k in range(KD):
                    m = pe.matmul(ps[0][:, NE * i:NE * i + NE], tokT[:, k, P * i:P * i + P], rw[:, k],
                                  start=k == 0, stop=k == KD - 1)
            m.then_inc(s["lgt"], 1)

            def ple(n):
                if n == 0:
                    pe.wait_ge(d_ple, 48)
                    pe.wait_ge(s["lg"], 2)
                i, hh = n // 2, n % 2
                for k in range(2):
                    m = pe.matmul(ps[n][:], pt[:, k, P * i:P * i + P], wple[:, k, 512 * hh:512 * hh + 512],
                                  start=k == 0, stop=k == 1)
                m.then_inc(s["eraw"], 1)

            ple(0)
            ple(1)
            pe.wait_ge(s["cnt"], 2)
            pe.matmul(ps[6][:, 0:NE], mat("tri"), gt[:, 0], start=True, stop=True)
            pe.matmul(ps[6][:, NE:2 * NE], ones, gt[:, 0], start=True, stop=False)
            pe.matmul(ps[6][:, NE:2 * NE], mat("tri"), gt[:, 1], start=False, stop=True)
            for i in range(TI):
                m = pe.matmul(ps[7][0:NE, 0:1], gt[:, i], ones[:, 0:1], start=i == 0, stop=i == 1)
            m.then_inc(s["pos"], 1)
            ple(2)
            pe.wait_ge(s["start"], 1)
            pe.matmul(ps[7][0:NE, 2:4], mat("tri", NE)[:, 0:NE], blocks_used, start=True, stop=True)
            pe.matmul(ps[7][0:1, 64:64 + NE], ne_, mat("tri32i", NE), start=True, stop=True).then_inc(s["tab"], 1)
            pe.wait_ge(s["wr"], 4)
            for i in range(TI):
                pe.transpose(ps[4][0:NE, P * i:P * i + P], ceq[:, i], ident)
                m = pe.transpose(ps[5][0:NE, P * i:P * i + P], ew[:, i], ident)
                m.then_inc(s["pwT"], 1)
            pe.wait_ge(s["tabv"], 2)
            pe.matmul(ps[7][0:1, 128:128 + NBT], load16, oh, start=True, stop=True).then_inc(s["row"], 1)
            for n in range(PARTS):
                m = pe.matmul(ps[7][NE * n:NE * n + NE, 256:256 + NBT], ident[0:NE, 0:NE], oh, start=True, stop=True)
            m.then_inc(s["row"], 1)
            pe.wait_ge(s["pwTs"], 2)
            for i in range(TI):
                pe.matmul(ps[6][:, 64 + NBT * i:64 + NBT * i + NBT], pwT[:, 0, P * i:P * i + P], oh,
                          start=True, stop=False)
                pe.matmul(ps[6][:, 64 + NBT * i:64 + NBT * i + NBT], mat("ones", NE), ohs, start=False, stop=True)
                m = pe.matmul(ps[6][:, 192 + NBT * i:192 + NBT * i + NBT], pwT[:, 1, P * i:P * i + P], oh,
                              start=True, stop=True)
            m.then_inc(s["pb"], 1)
            ple(3)

            def gather():
                for k in range(KD):
                    for i in range(TI):
                        for n in range(PARTS):
                            m = pe.matmul(ps[6][:, SLOTS * k:SLOTS * k + SLOTS], tok3[n][:, i, P * k:P * k + P],
                                          sel[:, i], start=i + n == 0, stop=i * n == (TI - 1) * (PARTS - 1))
                m.then_inc(s["gx"], 1)

            def scatter(done=None):
                for n in range(4):
                    i = n // 2
                    hh = slice(64 * (n % 2), 64 * (n % 2) + 64)
                    m = pe.matmul(ps[n][:], selwT[hh, P * i:P * i + P], y[hh, :], start=False, stop=False,
                                  skip_group_check=True)
                    if done is not None:
                        m.then_inc(done, 1)

            pe.wait_ge(s["sel"], 1)
            pe.wait_ge(s["tok3"], 1)
            gather()
            pe.wait_ge(s["ers"], 4)
            pe.wait_ge(d_bdn, 16)
            for n in range(4):
                m = pe.matmul(ps[n][:], pwT[:, 1, P * (n // 2):P * (n // 2) + P], bdn[:, 512 * (n % 2):512 * (n % 2) + 512],
                              start=True, stop=False, skip_group_check=True)
            m.then_inc(s["accfree"], 1)
            pe.wait_ge(s["bias3"], 1)

            pe.wait_ge(s["tabr"], 2)
            blocks = pe.value_load(table[0:1, TE + NE - 1:TE + NE], min_val=0, max_val=CHUNKS * NB)
            with pe.Fori(0, NB) as b:
                with pe.If(b * CHUNKS <= blocks):
                    loaded = pe.value_load(table[0:1, bass.ds(b + TB, 1)], min_val=16, max_val=16 * NE)
                    pe.wait_ge(s["gxs"], b + 1)
                    pe.wait_ge(s["onehot"], b + 1)
                    for bk in (4, 5):
                        for hh in range(2):
                            at = D * (bk - 4) + 512 * hh
                            pe.matmul(ps[bk][64 * hh:64 * hh + 64, :], onehot, bias3[:, at:at + 512],
                                      start=True, stop=False)
                    for c in range(4):
                        for bk in (4, 5):
                            slot = 2 * c + bk - 4
                            pe.wait_ge(d_w[slot], loaded)
                            for j in range(2):
                                k = 2 * c + j
                                for hh in range(2):
                                    m = pe.matmul(ps[bk][64 * hh:64 * hh + 64, :], xg[:, SLOTS * k:SLOTS * k + SLOTS],
                                                  wslot[slot][:, j, 512 * hh:512 * hh + 512],
                                                  start=False, stop=k == KD - 1)
                            m.then_inc(s["used"], 1)
                    pe.wait_ge(s["ye"], b * CHUNKS + CHUNKS)
                    scatter()
                    pe.wait_ge(s["sel"], b + 2)
                    pe.wait_ge(s["g"], b + 1)
                    for i in range(TI):
                        m = pe.transpose(ps[4][:, P * i:P * i + P], selw[:, i], ident)
                    m.then_inc(s["sT"], 1)
                    pe.wait_ge(s["a"], b + 1)
                    for j in range(4):
                        m = pe.transpose(ps[5][:, P * j:P * j + P], act[:, P * j:P * j + P], ident)
                    m.then_inc(s["aTt"], 1)
                    gather()
                    pe.wait_ge(s["sTs"], b + 1)
                    pe.wait_ge(s["aTe"], b + 1)
                    for c in range(4):
                        pe.wait_ge(d_w[8 + c], loaded)
                        for j in range(2):
                            k = 2 * c + j
                            at = P * (k % 4) + SLOTS * (k // 4)
                            for hh in range(2):
                                m = pe.matmul(ps[7][64 * hh:64 * hh + 64, :], actT[:, at:at + SLOTS],
                                              wslot[8 + c][:, j, 512 * hh:512 * hh + 512], start=k == 0, stop=k == KD - 1)
                        m.then_inc(s["used"], 1)
            pe.wait_ge(s["ye"], blocks + 2 * CHUNKS)
            scatter(s["scat"])

            for n in range(4):
                for k in (2 * n, 2 * n + 1):
                    for i in range(TI):
                        pe.wait_ge(s["h2"], 2 * i + 2)
                        m = pe.transpose(ps[4 + n][:, 256 * (k % 2) + P * i:256 * (k % 2) + P * i + P],
                                         h[:, i, P * k:P * k + P], ident)
                m.then_inc(s["h2T"], 1)
            pe.wait_ge(d_tail, 32)
            pe.wait_ge(d_wpg, 16)
            pe.wait_ge(s["h2Ts"], 4)
            for n in range(4):
                i, hh = n // 2, n % 2
                pe.matmul(ps[n][:], mat("ones", 1), bple[0:1, 512 * hh:512 * hh + 512], start=True, stop=False)
                for k in range(KD):
                    m = pe.matmul(ps[n][:], hT[:, k, P * i:P * i + P], wpg[:, k, 512 * hh:512 * hh + 512],
                                  start=False, stop=k == KD - 1)
                m.then_inc(s["gate"], 1)

        @block.vector
        def _(dve):
            chain = [0]

            def link(ins):
                chain[0] += 1
                ins.then_inc(s["V"], 1)
                dve.wait_ge(s["V"], chain[0])

            def flt_arg(n):
                dve.wait_ge(s["f1"], n + 1)
                bb = col("b1", 0, 1, FO) if n == 0 else col("binner", n - 1, 1, FO)
                x0, kk = fargs[:, 0], fargs[:, 1]
                if n:
                    dve.wait_ge(s["fs"], n)
                link(dve.tensor_scalar(x0, ps[5][0:FO, 0:S], bb, col("freq", n, 1, FO), ALU.add, ALU.mult))
                link(dve.tensor_scalar(kk, x0, 1.0 / (2 * math.pi), ROUND, ALU.mult, ALU.add))
                link(dve.tensor_scalar(kk, kk, ROUND, None, ALU.subtract))
                for c in TWO_PI:
                    link(dve.scalar_tensor_tensor(x0, kk, -c, x0, ALU.mult, ALU.add))
                dve.tensor_scalar(x0, x0, PI_BELOW, -PI_BELOW, ALU.min, ALU.max).then_inc(s["fa"], 1)

            dve.wait_ge(s["std"], 1)
            link(dve.reciprocal(rstd, std))
            for i in range(TI):
                dve.tensor_scalar(xn[:, i], h[:, i], rstd[:, i:i + 1], None, ALU.mult).then_inc(s["xn"], 1)
            flt_arg(0)
            for k in (0, 1, 4, 5):
                dve.wait_ge(s["xT"], k // 2 + 1)
                dve.tensor_scalar(aT[:, k], half(k // 2, k % 2), col("gmix", k), None, ALU.mult).then_inc(s["aTv"], 1)
            dve.tensor_tensor(lamp, col("lq", 0, 2, FO), col("lk", 0, 2, FO), ALU.mult).then_inc(s["lam"], 1)
            dve.tensor_scalar(subl, col("subln"), 1.0 - LAMBDA_INIT, None, ALU.mult).then_inc(s["lam"], 1)
            flt_arg(1)

            def apply_rope(dst, b0, turned, done):
                dve.wait_ge(s[turned], 1)
                dve.wait_ge(d_rope, 16)
                if dst is qrope:
                    dve.wait_ge(s["xT"], 4)
                for c in range(2):
                    m = dve.tensor_tensor(dst[:, 2 * c:2 * c + 2], ps[b0 + c][:].rearrange("p (c t) -> p c t", c=2),
                                          rope[:, 1:2].to_broadcast([P, 2, S]), ALU.mult)
                link(m)
                link(dve.tensor_tensor(raw, raw, rope[:, 0:1].to_broadcast([P, H, S]), ALU.mult))
                dve.tensor_tensor(dst, dst, raw, ALU.add).then_inc(s[done], 1)

            apply_rope(qrope, 0, "rotq", "qr")
            flt_arg(2)
            apply_rope(krope, 2, "rotk", "kr")

            dve.wait_ge(s["lame"], 1)
            link(dve.tensor_tensor(nlam, lame[:, 1:2], lame[:, 0:1], ALU.subtract))
            link(dve.tensor_scalar(nlam, nlam, LAMBDA_INIT, None, ALU.subtract))

            def decayed(side):
                dst = (ffwd, fbwd)[side]
                for i in range(TI):
                    dve.wait_ge(s["fo"], 2 * side + i + 1)
                    if side == 1:
                        dve.wait_ge(s["fo"], 4)
                    dve.tensor_tensor(dst[:, i], ps[4 + i][:], decay[:, i], ALU.mult).then_inc(s["fd"], 1)

            def conv_rest(n):
                dst = (hv, hx1, hx0)[n // 2]
                dve.wait_ge(s["projs"], 2 * n + 2)
                for c in range(2):
                    ct = 4 * (GROUPS[3 + n // 2] - 3) + 2 * (n % 2) + c
                    x, yy = half(6 + n % 2, c), dst[:, ct % 4]
                    link(dve.scalar_tensor_tensor(yy[:, 1:S], x[:, 0:S - 1], col("cw", ct), yy[:, 1:S],
                                                  ALU.mult, ALU.add))
                    chain[0] += 1
                    dve.scalar_tensor_tensor(yy[:, 0:S - 1], x[:, 1:S], col("cw", 24 + ct), yy[:, 0:S - 1],
                                             ALU.mult, ALU.add).then_inc(s["conv"], 1)
                    chain[0] -= 1

            def maxima(hd):
                sl = hd % 2
                dve.wait_ge(s["sc"], hd + 1)
                for c in range(2):
                    at = 4 * sl + 2 * c
                    m = dve.tensor_reduce(mx[:, at:at + 2], ps[2 * sl + c][:].rearrange("p (i k) -> p i k", i=2),
                                          AX.X, ALU.max)
                link(m)
                dve.tensor_scalar(nmx[:, 4 * sl:4 * sl + 4], mx[:, 4 * sl:4 * sl + 4], -SCALE, None, ALU.mult
                                  ).then_inc(s["nmx"], 1)

            def difference(hd):
                sl = hd % 2
                at = 4 * sl
                dve.wait_ge(s["ex"], 4 * hd + 4)
                link(dve.reciprocal(rsi[:, at:at + 4], rs[:, at:at + 4]))
                link(dve.tensor_scalar(rsi[:, at + 2:at + 4], rsi[:, at + 2:at + 4], nlam, None, ALU.mult))
                for i in range(TI):
                    m = dve.tensor_scalar(E[:, sl, 1, i], E[:, sl, 1, i], rsi[:, at + 2 + i:at + 3 + i], None, ALU.mult)
                link(m)
                for i in range(TI):
                    m = dve.scalar_tensor_tensor(E[:, sl, 0, i], E[:, sl, 0, i], rsi[:, at + i:at + i + 1],
                                                 E[:, sl, 1, i], ALU.mult, ALU.add)
                m.then_inc(s["df"], 1)

            dve.wait_ge(d_dec, 16)
            dve.wait_ge(s["fs"], 3)
            decayed(0)
            conv_rest(0)
            maxima(0)
            decayed(1)
            conv_rest(1)
            difference(0)
            maxima(1)
            conv_rest(2)
            difference(1)
            conv_rest(3)
            dve.wait_ge(s["conv"], 8)
            for c in range(4):
                dve.tensor_tensor(hv[:, c], hv[:, c], hx1[:, c], ALU.mult).then_inc(s["u"], 1)
            maxima(2)
            conv_rest(4)
            difference(2)
            maxima(3)
            conv_rest(5)
            dve.wait_ge(s["nys"], 1)
            for f in range(TI):
                dve.wait_ge(s["ur"], f + 1)
                dve.wait_ge(s["ui"], f + 1)
                if f:
                    dve.wait_ge(s["Y"], 2)
                ur, ui = ps[4 + f][:], ps[6 + f][:]
                dve.tensor_tensor(prod[:, 0], ur, Kre[:, f], ALU.mult).then_inc(s["pr"], 1)
                dve.tensor_tensor(prod[:, 1], ui, Kim[:, f], ALU.mult).then_inc(s["pr"], 1)
                dve.tensor_tensor(prod[:, 2], ur, Kim[:, f], ALU.mult).then_inc(s["pr"], 1)
                dve.tensor_tensor(prod[:, 3], ui, Kre[:, 1] if f else K0, ALU.mult).then_inc(s["pr"], 1)
            difference(3)
            for n in range(2):
                dve.wait_ge(s["rsa"], n + 1)
                link(dve.reciprocal(rsa[:, 2 * n:2 * n + 2], rsa[:, 2 * n:2 * n + 2]))
                if n == 0:
                    dve.wait_ge(s["proj"], 12)
                for hd in (2 * n, 2 * n + 1):
                    dve.scalar_tensor_tensor(mixT[:, hd], o[:, hd], subl, rsa[:, hd], ALU.mult, ALU.mult
                                             ).then_inc(s["mixa"], 1)
            dve.wait_ge(s["uT"], 2)
            for c in range(4):
                dve.wait_ge(s["yi"], 2 * (c // 2) + 2)
                link(dve.scalar_tensor_tensor(z[:, c], hv[:, c], col("dskip", c), half(1 + 2 * (c // 2), c % 2),
                                              ALU.mult, ALU.add))
                dve.tensor_tensor(z[:, c], z[:, c], hx0[:, c], ALU.mult).then_inc(s["z"], 1)
            dve.wait_ge(s["z"], 4)
            for n in range(2):
                dve.wait_ge(s["rsh"], n + 1)
                link(dve.reciprocal(rsh[:, 2 * n:2 * n + 2], rsh[:, 2 * n:2 * n + 2]))
                for c in (2 * n, 2 * n + 1):
                    dve.scalar_tensor_tensor(mixT[:, 4 + c], z[:, c], col("gn", c), rsh[:, c], ALU.mult, ALU.mult
                                             ).then_inc(s["mixh"], 1)
            for n, bk in enumerate((0, 2, 6, 7)):
                i, hh = n // 2, n % 2
                dve.wait_ge(s["mix"], n + 1)
                hp = h[:, i, 512 * hh:512 * hh + 512]
                dve.tensor_tensor(hp, ps[bk][:], hp, ALU.add).then_inc(s["hres"], 1)

            dve.wait_ge(d_gffn, 16)
            for i in range(TI):
                dve.wait_ge(s["hstd"], i + 1)
                link(dve.reciprocal(rstd[:, i:i + 1], std[:, i:i + 1]))
                dve.scalar_tensor_tensor(tok[:, i], h[:, i], rstd[:, i:i + 1], gffn, ALU.mult, ALU.mult
                                         ).then_inc(s["tok"], 1)
            dve.wait_ge(s["lgt"], 1)
            for i in range(TI):
                m = dve.tensor_tensor(lg[:, i], ps[0][:, NE * i:NE * i + NE], rb[:], ALU.add)
                m.then_inc(s["lg"], 1)
            dve.wait_ge(s["lg"], 2)
            for i in range(TI):
                m = dve.max(m8[:, i], lg[:, i])
            link(m)
            for i in range(TI):
                dve.tensor_scalar(nm1[:, i:i + 1], m8[:, i, 0:1], -1.0, None, ALU.mult).then_inc(s["nm1"], 1)
            for i in range(TI):
                v4 = m8[:, i, TOPK - 1:TOPK]
                dve.tensor_scalar(gt[:, i], lg[:, i], v4, None, ALU.is_gt, ALU.add, accum_out=need[:, i:i + 1])
                m = dve.tensor_scalar(eq[:, i], lg[:, i], v4, None, ALU.is_equal)
            link(m)
            link(dve.tensor_scalar(need, need, -1.0, float(TOPK), ALU.mult, ALU.add))
            for i in range(TI):
                m = dve.tensor_tensor_scan(ceq[:, i], mat("ones")[:, 0:NE], eq[:, i], 0.0, ALU.mult, ALU.add)
            link(m)
            for i in range(TI):
                m = dve.scalar_tensor_tensor(eq[:, i], ceq[:, i], need[:, i:i + 1], eq[:, i], ALU.is_le, ALU.mult)
            link(m)
            for i in range(TI):
                dve.tensor_tensor(gt[:, i], gt[:, i], eq[:, i], ALU.add).then_inc(s["cnt"], 1)
            dve.wait_ge(s["cnt"], 2)
            dve.wait_ge(s["ew"], 2)
            for i in range(TI):
                m = dve.scalar_tensor_tensor(ew[:, i], gt[:, i], 1.0, ew[:, i], ALU.mult, ALU.mult,
                                             accum_out=wsum[:, i:i + 1])
            link(m)
            link(dve.reciprocal(winv, wsum))
            dve.wait_ge(s["pos"], 1)
            cnt = ps[7][0:NE, 0:1]
            link(dve.tensor_scalar(nonempty, cnt, 0.0, col("first", 0, 1, NE), ALU.is_gt, ALU.max))
            link(dve.tensor_scalar(ne_, cnt, float(SLOTS), nonempty, ALU.is_gt, ALU.add))
            link(dve.tensor_scalar(c1, cnt, float(2 * SLOTS), ne_, ALU.is_gt, ALU.add))
            dve.tensor_scalar(ne_, cnt, float(3 * SLOTS), c1, ALU.is_gt, ALU.add).then_inc(s["start"], 1)
            for i in range(TI):
                dve.tensor_scalar(ew[:, i], ew[:, i], winv[:, i:i + 1], None, ALU.mult).then_inc(s["wr"], 1)
                m = dve.scalar_tensor_tensor(ceq[:, i], ps[6][:, NE * i:NE * i + NE], FAR, gt[:, i], ALU.add, ALU.mult)
            link(m)
            for i in range(TI):
                dve.tensor_scalar(ceq[:, i], ceq[:, i], FAR, None, ALU.subtract).then_inc(s["wr"], 1)
            dve.wait_ge(s["tab"], 1)
            link(dve.tensor_copy(starts, ps[7][0:NE, 2:4]))
            link(dve.tensor_scalar(load16, before_, 16.0, 16.0, ALU.mult, ALU.add))
            dve.tensor_scalar(table[0:1, TE:TE + NE], ps[7][0:1, 64:64 + NE], float(CHUNKS), -float(CHUNKS),
                              ALU.mult, ALU.add).then_inc(s["tabr"], 1)
            dve.wait_ge(s["tabr"], 1)
            link(dve.tensor_tensor(en_, st_, ne_, ALU.add))
            link(dve.tensor_scalar(ohs, mat("blkno", NE), st_, None, ALU.is_ge))
            dve.scalar_tensor_tensor(oh, mat("blkno", NE), en_, ohs, ALU.is_lt, ALU.mult).then_inc(s["tabv"], 1)
            dve.wait_ge(s["tabv"], 1)
            dve.tensor_scalar(ohs, oh, st_, float(SLOTS), ALU.mult, ALU.mult).then_inc(s["tabv"], 1)
            dve.wait_ge(s["row"], 2)
            dve.tensor_copy(table[0:1, TB:TB + NBT], ps[7][0:1, 128:128 + NBT]).then_inc(s["tabr"], 1)
            link(dve.tensor_copy(oh3[:, 0:NBT], ps[7][0:PARTS * NE, 256:256 + NBT]))
            dve.tensor_scalar(onehot, mat("ones")[0:PARTS * NE, 0:SLOTS], oh3[:, 0:1], None, ALU.mult
                              ).then_inc(s["onehot"], 1)
            dve.wait_ge(s["pb"], 1)
            for i in range(TI):
                dve.tensor_tensor(posb[:, i], ps[6][:, 64 + NBT * i:64 + NBT * i + NBT], mat("blk64"), ALU.subtract)
                m = dve.tensor_copy(wb[:, i], ps[6][:, 192 + NBT * i:192 + NBT * i + NBT])
            link(m)
            for i in range(TI):
                m = dve.tensor_scalar(sel[:, i], mat("slot2")[:, 0:SLOTS], posb[:, i, 0:1], None, ALU.is_equal)
            m.then_inc(s["sel"], 1)
            dve.wait_ge(s["estd"], 1)
            link(dve.reciprocal(rstd, std))
            for i in range(TI):
                dve.scalar_tensor_tensor(e[:, i], e[:, i], rstd[:, i:i + 1], gple, ALU.mult, ALU.mult
                                         ).then_inc(s["en"], 1)

            dve.wait_ge(s["tabr"], 2)
            blocks = dve.value_load(table[0:1, TE + NE - 1:TE + NE], min_val=0, max_val=CHUNKS * NB)
            with dve.Fori(0, NB) as b:
                with dve.If(b * CHUNKS <= blocks):
                    dve.wait_ge(s["gx"], b + 1)
                    for i in range(TI):
                        dve.tensor_scalar(selw[:, i], mat("slot2"), posb[:, i, bass.ds(b, 1)], wb[:, i, bass.ds(b, 1)],
                                          ALU.is_equal, ALU.mult)
                    for i in range(TI):
                        m = dve.tensor_scalar(sel[:, i], mat("slot2")[:, 0:SLOTS], posb[:, i, bass.ds(b + 1, 1)], None,
                                              ALU.is_equal)
                    m.then_inc(s["sel"], 1)
                    dve.wait_ge(s["used"], b * CHUNKS + 8)
                    dve.tensor_scalar(g, ps[4][:], LIMIT, None, ALU.min).then_inc(s["g"], 1)
                    dve.tensor_scalar(u, ps[5][:], LIMIT, -LIMIT, ALU.min, ALU.max).then_inc(s["uc"], 1)
                    dve.wait_ge(s["uc"], b * 2 + 1)
                    dve.scalar_tensor_tensor(u, u, 1.0, g, ALU.add, ALU.mult).then_inc(s["uc"], 1)
                    dve.wait_ge(s["uc"], b * 2 + 2)
                    dve.wait_ge(s["sg"], b + 1)
                    dve.tensor_tensor(act, u, sg, ALU.mult).then_inc(s["a"], 1)
                    dve.tensor_scalar(onehot, mat("ones")[0:PARTS * NE, 0:SLOTS], oh3[:, bass.ds(b + 1, 1)], None,
                                      ALU.mult).then_inc(s["onehot"], 1)

            for n in range(4):
                dve.wait_ge(s["scat"], n + 1)
                hp = h[:, n // 2, 512 * (n % 2):512 * (n % 2) + 512]
                dve.tensor_tensor(hp, ps[n][:], hp, ALU.add).then_inc(s["h2"], 1)
            for n in range(4):
                i, hh = n // 2, n % 2
                cs = slice(512 * hh, 512 * hh + 512)
                dve.wait_ge(s["gsig"], n + 1)
                link(dve.tensor_tensor(e[:, i, cs], tok[:, i, cs], e[:, i, cs], ALU.mult))
                dve.tensor_tensor(h[:, i, cs], h[:, i, cs], e[:, i, cs], ALU.add).then_inc(s["gm"], 1)
            dve.wait_ge(d_tail, 32)
            for i in range(TI):
                dve.wait_ge(s["fstd"], i + 1)
                link(dve.reciprocal(rstd[:, i:i + 1], std[:, i:i + 1]))
                dve.scalar_tensor_tensor(tok[:, i], h[:, i], rstd[:, i:i + 1], gfin, ALU.mult, ALU.mult
                                         ).then_inc(s["fin"], 1)


def shape_constants():
    f32 = np.float32
    t = np.arange(S)
    ang = 2 * np.pi * np.outer(t, t) / NFFT
    cosf = np.cos(ang)
    sink = -np.sin(ang)
    sinu = sink.copy()
    sinu[:, 0] = (-1.0) ** t
    dft = np.stack([cosf, sinu, sink, sinu.T]).astype(f32)
    inv = f32(10000.0) ** (-np.arange(0, DH, 2, dtype=f32) / f32(DH))
    rot_ang = (np.arange(S, dtype=f32)[:, None] * inv[None, :]).astype(f32)
    rope = np.stack([np.tile(np.cos(rot_ang).T, (4, 1)), np.tile(np.sin(rot_ang).T, (4, 1))], 1).astype(f32)
    pos = np.arange(S, dtype=f32)
    tt = (pos / f32(S - 1)).astype(f32)
    bands = (EMB - 1) // 2
    f = np.linspace(1e-4, bands - 1, bands, dtype=f32)
    fw = (((f32(2.0 * math.pi / S)) * pos)[:, None] * f[None, :]).astype(f32)
    zt = np.concatenate([tt[:, None], np.cos(fw), -np.sin(fw)], axis=-1).astype(f32).T
    lo, hi = math.log(1e-2) / 1.5, math.log(1e-2) / 0.3
    deltas = np.abs(np.linspace(lo, hi, HW, dtype=f32))
    decay = np.exp(-tt[:, None] * deltas[None, :]).astype(f32)
    c = {}
    c["cf"] = np.full((P, TI), 2.0 / NFFT)
    c["cf"][0, 0] = 1.0 / NFFT
    c["eps6"] = np.full((P, 1), 1e-6)
    c["eps5"] = np.full((P, 1), 1e-5)
    c["first"] = np.arange(P)[:, None] == 0
    c["ident"] = np.eye(P)
    r = np.zeros((P, P))
    for m in range(P):
        if m % 64 < 32:
            r[m + 32, m] = -1.0
        else:
            r[m - 32, m] = 1.0
    c["rot"] = r
    c["blk"] = np.kron(np.eye(2), np.ones((64, 64)))
    c["tri"] = np.triu(np.ones((P, P)), 1)
    c["ones"] = np.ones((P, P))
    c["slot2"] = np.tile(np.arange(SLOTS), (P, 2))
    c["blkno"] = np.tile(np.arange(NBT), (P, 1))
    c["blk64"] = SLOTS * c["blkno"]
    c["tri32i"] = np.triu(np.ones((P, NE)))
    return dft, rope, zt, decay, {k: np.asarray(v_, f32) for k, v_ in c.items()}


def kernel(**inputs):
    import concourse.bacc as bacc
    from concourse.bass_utils import run_bass_kernel_spmd as run

    dft, rope, zt, decay, c = shape_constants()
    given = {k: np.asarray(v_) for k, v_ in inputs.items()}

    def per_partition(vec, n):
        return vec.reshape(n, P).T

    def on_64(rows):
        return np.concatenate([rows.T, rows.T], axis=0)

    c["gmix"] = per_partition(given["g_mix"][0], KD)
    c["cw"] = np.concatenate([per_partition(given["hyena_conv_w"][0, j], 12) for j in range(3)], axis=1)
    c["cb"] = per_partition(given["hyena_conv_b"][0], 12)
    c["dskip"] = per_partition(given["hyena_d"][0], 4)
    c["gn"] = per_partition(given["hyena_gn"][0], 4)
    c["subln"] = given["attn_subln"][0].reshape(P, 1)
    c["b1"] = on_64(given["flt_b1"])
    c["binner"] = on_64(given["flt_b_inner"][0])
    c["freq"] = on_64(given["flt_freq"][0])
    c["lq"] = on_64(np.concatenate([given["lambda_q1"], given["lambda_q2"]], axis=0))
    c["lk"] = on_64(np.concatenate([given["lambda_k1"], given["lambda_k2"]], axis=0))
    arrays = {
        "cols": np.concatenate([c[n] for n in COLS], axis=1),
        "rope": rope, "dft": dft, "decay": decay, "zt": zt,
        "pt": given["p"][0, 0].T,
    }
    nc = bacc.Bacc("TRN2", target_bir_lowering=False, num_devices=1)
    feeds, aps = {}, {}
    for name in INPUTS:
        arr = np.ascontiguousarray(arrays[name] if name in arrays else given[name])
        feeds["in_" + name] = arr
        aps[name] = nc.dram_tensor("in_" + name, arr.shape, mybir.dt.from_np(arr.dtype), kind="ExternalInput").ap()
    out = nc.dram_tensor("out", (1, S, D), F32, kind="ExternalOutput").ap()
    build(nc, aps, out)
    r = run(nc, [feeds], core_ids=[0])
    return r.results[0]["out"]
```

```python
import math
from contextlib import ExitStack

import numpy as np

import concourse.bass as bass
from concourse import mybir

F32 = mybir.dt.float32
BF16 = mybir.dt.bfloat16
I32 = mybir.dt.int32
ALU = mybir.AluOpType
ACT = mybir.ActivationFunctionType
AX = mybir.AxisListType

P = 128
D = 1024
S = 256
TI = S // P
KD = D // P
HW = 512
H = 4
DH = 64
SCALE = DH ** -0.5
LAMBDA_INIT = 0.8 - 0.6 * math.exp(0.0)
NFFT = 2 * S
EMB = 33
FO = 64
NE = 32
TOPK = 4
ALPHA = 1.702
LIMIT = 7.0
SLOTS = 64
NB = NE + (S * TOPK - NE) // SLOTS
LAP = 8
NBT = NB + LAP
CHUNKS = 12
TWICE = 4
PARTS = 3
SHARED = 23200
GROUPS = (0, 1, 2, 3, 5, 4)
FAR = 4096.0
ROUND = 12582912.0
TWO_PI = (6.28125, 0.0019350051879882812, 3.0199159819567e-07)
PI_BELOW = 3.1415925

COLS = {}
for _name, _n in (("gmix", KD), ("gffn", KD), ("cw", 36), ("cb", 12), ("dskip", 4), ("gn", 4), ("subln", 1), ("b1", 1),
                  ("binner", 2), ("freq", 3), ("lq", 2), ("lk", 2), ("cf", TI), ("eps6", 1), ("eps5", 1),
                  ("first", 1), ("ident", P), ("rot", P), ("blk", P), ("tri", P), ("ones", P),
                  ("slot2", 2 * SLOTS), ("blkno", NBT), ("blk64", NBT), ("tri32i", NE)):
    COLS[_name] = (sum(n for _, n in COLS.values()), _n)
NCOLS = sum(n for _, n in COLS.values())

INPUTS = ["x", "cols", "rope", "dft", "decay", "zt", "w_in", "flt_w1", "flt_w_inner", "flt_w_out", "w_out",
          "g_ffn", "router_w", "router_b", "w_gate", "b_gate", "w_up", "b_up", "w_down", "b_down",
          "pt", "w_ple", "g_ple", "w_ple_gate", "b_ple_gate", "g_final"]


def build(nc, a, out):
    with ExitStack() as ctx:
        def sb(name, shape, dt=F32):
            return ctx.enter_context(nc.sbuf_tensor(name, shape, dt))

        def sem(name):
            return ctx.enter_context(nc.semaphore(name))

        ring = sb("ring", [P, 12, 2048])
        h = sb("h", [P, TI, D])
        cols = sb("cols", [P, NCOLS])
        small = sb("small", [P, 256])
        rw = sb("rw", [P, KD, NE])
        rb = sb("rb", [P, NE])
        shared = sb("shared", [P, SHARED])

        def col(name, i=0, n=1, p=P):
            at = COLS[name][0] + i
            return cols[0:p, at:at + n]

        def mat(name, p=P):
            at, n = COLS[name]
            return cols[0:p, at:at + n]

        used = {"f": 0, "m": 0}

        def part(phase, n, p=P):
            at = used[phase]
            used[phase] += n
            assert used[phase] <= SHARED, used
            return shared[0:p, at:at + n]

        aT = part("f", 2048).rearrange("p (k t) -> p k t", k=KD)
        mixT = aT
        xn = part("f", 2048).rearrange("p (i d) -> p i d", i=TI)
        qrope = xn[:, 0].rearrange("p (c t) -> p c t", c=H)
        krope = xn[:, 1].rearrange("p (c t) -> p c t", c=H)
        raw = part("f", 1024).rearrange("p (c t) -> p c t", c=H)
        v = part("f", 1024).rearrange("p (i n) -> p i n", i=TI)
        E = part("f", 2048).rearrange("p (s c i k) -> p s c i k", s=2, c=2, i=TI)
        diffT = part("f", 1024).rearrange("p (s j q) -> p s j q", s=2, j=TI)
        o = raw
        hv = part("f", 1024).rearrange("p (c t) -> p c t", c=4)
        hx1 = part("f", 1024).rearrange("p (c t) -> p c t", c=4)
        hx0 = part("f", 1024).rearrange("p (c t) -> p c t", c=4)
        utm = part("f", 1024).rearrange("p (i c) -> p i c", i=TI)
        Kre = part("f", 1024).rearrange("p (i c) -> p i c", i=TI)
        Kim = part("f", 1024).rearrange("p (i c) -> p i c", i=TI)
        K0 = part("f", 512)
        rope = K0.rearrange("p (c t) -> p c t", c=2)
        prod = part("f", 2048).rearrange("p (n c) -> p n c", n=4)
        Yre = part("f", 1024).rearrange("p (i c) -> p i c", i=TI)
        Yim = part("f", 1024).rearrange("p (i c) -> p i c", i=TI)
        ffwd = prod[:, 0:2]
        fbwd = prod[:, 2:4]
        fsum = Yre
        fdif = Yim
        decay = utm
        cosf = part("f", 512).rearrange("p (i f) -> p i f", i=TI)
        sinu = part("f", 512).rearrange("p (i f) -> p i f", i=TI)
        sink = part("f", 512).rearrange("p (i f) -> p i f", i=TI)
        sing = part("f", 512).rearrange("p (i f) -> p i f", i=TI)
        fargs = ffwd.rearrange("p n c -> p (n c)")[0:FO, 0:768].rearrange("p (n t) -> p n t", n=3)
        fh = fbwd.rearrange("p n c -> p (n c)")[0:FO, 0:768].rearrange("p (n t) -> p n t", n=3)
        wf1 = part("f", FO, EMB)
        zt = part("f", S, EMB)
        wfi = part("f", 2 * FO, FO).rearrange("p (j n) -> p j n", j=2)
        wfo = Kim.rearrange("p i c -> p (i c)")[0:FO]
        sqa = E.rearrange("p s c i k -> p (s c i k)")[:, 0:1024].rearrange("p (c t) -> p c t", c=H)
        rsa = E.rearrange("p s c i k -> p (s c i k)")[:, 1024:2048].rearrange("p (c t) -> p c t", c=H)
        z = hv
        sqh = utm.rearrange("p i c -> p (i c)").rearrange("p (c t) -> p c t", c=4)
        rsh = prod[:, 0:2].rearrange("p n c -> p (n c)").rearrange("p (c t) -> p c t", c=4)

        def place(at, n, p=P):
            assert at + n <= SHARED, at
            return shared[0:p, at:at + n]

        bple, gfin = place(0, D), place(D, D)
        hT = place(16384, 2048).rearrange("p (k t) -> p k t", k=KD)
        tokT = [place(at, D).rearrange("p (k t) -> p k t", k=KD) for at in (6144, 7168)]
        tok = place(2048, 2048).rearrange("p (i d) -> p i d", i=TI)
        e = [place(5120, D), place(8192, D)]
        wother = [place(at, 2 * D).rearrange("p (j n) -> p j n", j=2) for at in (6144, 9216, 11264, 13312)]
        gffn = place(10240, D)
        squares = place(15360, D)
        g, u = place(15360, 512), place(15872, 512)
        sg, act, actT = (place(at, 512) for at in (16384, 16896, 17408))
        y = place(17920, 512)
        xg = place(18688, 512)
        sel = place(19200, SLOTS).bitcast(BF16).rearrange("p (i s) -> p i s", i=TI)
        selw = place(19264, 4 * SLOTS).rearrange("p (i s) -> p i s", i=TI)
        sel2 = place(19520, 2 * SLOTS).bitcast(BF16).rearrange("p (i s) -> p i s", i=TI)
        selT = place(19648, S // 2).bitcast(BF16)
        ident16 = place(19776, P // 2).bitcast(BF16)
        slot_w = place(19840, 1)
        bdn = place(13312, D, NE)
        tok3 = [place(at, D).bitcast(BF16).rearrange("p (i d) -> p i d", i=TI) for at in (19968, 22016, 4096)]
        bias3 = place(20992, D, PARTS * NE).bitcast(BF16)
        bias_in = place(17920, 2 * D, PARTS * NE)

        def tiny(at, n, p=P):
            return small[0:p, at:at + n]

        ssq, std, rstd = tiny(0, 2), tiny(2, 2), tiny(4, 2)
        lamp, lame, nlam = tiny(6, 2, FO), tiny(8, 2), tiny(10, 1)
        subl = tiny(11, 1)
        mx, nmx, rs = tiny(12, 8), tiny(20, 8), tiny(28, 8)
        rsi = tiny(36, 8)
        fss = tiny(44, 4)
        rt = sb("rt", [P, 640])

        def rts(at, n, p=P):
            return rt[0:p, at:at + n]

        lg = rts(0, 64).rearrange("p (i e) -> p i e", i=TI)
        m8 = rts(64, 16).rearrange("p (i e) -> p i e", i=TI)
        gt = rts(80, 64).rearrange("p (i e) -> p i e", i=TI)
        eq = rts(144, 64).rearrange("p (i e) -> p i e", i=TI)
        ceq = rts(208, 64).rearrange("p (i e) -> p i e", i=TI)
        ew = rts(272, 64).rearrange("p (i e) -> p i e", i=TI)
        need, nm1, wsum, winv = rts(336, 2), rts(338, 2), rts(340, 2), rts(342, 2)
        blocks_used = rts(344, 2, NE)
        starts = rts(346, 2, NE)
        ne_, nonempty = blocks_used[:, 0:1], blocks_used[:, 1:2]
        st_, before_ = starts[:, 0:1], starts[:, 1:2]
        en_, c1, load16 = rts(348, 1, NE), rts(349, 1, NE), rts(350, 1, NE)
        first_slot = rts(639, 1, NE)
        pairs_, turns16, odd_ = rts(636, 1, NE), rts(637, 1, NE), rts(638, 1, NE)
        oh = rts(352, NBT, NE)
        ohs = rts(408, NBT, NE)
        oh3 = rts(574, (NBT + 1) // 2, PARTS * NE).bitcast(BF16)
        onehot = rts(604, SLOTS // 2, PARTS * NE).bitcast(BF16)
        posb = rts(464, 2 * NBT).rearrange("p (i b) -> p i b", i=TI)
        pwT = sb("pwT", [NE, 2, S])
        wb = sb("wb", [P, TI, NBT])
        y_big = [t.bitcast(BF16) for t in (place(18432, 256), rw[:].rearrange("p k n -> p (k n)"))]
        y_last = rts(64, 256).bitcast(BF16)
        y_mid = sb("y_mid", [P, 512], BF16)
        table = sb("table", [1, 3 * NBT + 2 * NE], I32)
        TB, TT, TO, TE, TP = 0, NBT, 2 * NBT, 3 * NBT, 3 * NBT + NE

        ps = [ctx.enter_context(nc.psum_tensor(f"bank{n}", [P, 512], F32)) for n in range(8)]

        AHEAD = 3

        def half(n, c):
            return ps[n][:, 256 * c:256 * c + 256]

        d_cols, d_flt, d_rope, d_dft, d_dec, d_rw = (sem(n) for n in (
            "d_cols", "d_flt", "d_rope", "d_dft", "d_dec", "d_rw"))
        d_x = [sem(f"d_x{i}") for i in range(TI)]
        d_win = [sem(f"d_win{n}") for n in range(6)]
        d_wout, d_ple, d_bdn, d_gains, d_tail, d_wpg = (sem(n) for n in (
            "d_wout", "d_ple", "d_bdn", "d_gains", "d_tail", "d_wpg"))
        d_bias = sem("d_bias")
        d_w = [sem(f"d_w{c}") for c in range(12)]
        d_wother = [sem(f"d_wother{c}") for c in range(TWICE)]
        names = ("V Y a aTe aTs aTt aTv cnt conv dT dTs df dout en eraw ers essq estd ew ex f1 fa fd fdif "
                 "fin fo fs fsq fstd fsum fsum2 g gate gm gsig gx gxs h2 h2T h2Ts h2Tv hi hres hsq hstd kim "
                 "kims kr kre kres lam lame lamp lgt load16 mix mixa mixh nm1 nmx ny nys o onehot opened pb "
                 "pos pr prep proj projs pv pwT pwTs qr rawk rawq rest rotk rotq row rsa rsh sT sTs sc scat "
                 "sel sg sna snh split sqa sqh ssq start std tT tTs tab tabr tabv tok u uT uc ui ur used uts "
                 "vv wr xT xn ye yhi yi yr z").split()
        s = {n: sem("s_" + n) for n in names}

        block = ctx.enter_context(nc.Block())
        wslot = [ring[:, c].rearrange("p (j n) -> p j n", j=2) for c in range(12)]
        win = [ring[:, 2 * n:2 * n + 2].rearrange("p a n -> p (a n)").rearrange("p (k n) -> p k n", k=KD)
               for n in range(6)]
        wout = ring[:, 8:12].rearrange("p a n -> p (a n)").rearrange("p (k n) -> p k n", k=KD)

        def expert_rows(w, ex, c):
            return w[0, ex, 256 * c:256 * c + 256].rearrange("(j p) n -> p j n", p=P)

        def next_expert_rows(w, ex, c):
            return w[0, 1:NE][bass.ds(ex, 1), 256 * c:256 * c + 256].rearrange("a (j p) n -> p (a j) n", p=P)

        wple = wslot[0]
        pt = wslot[1][:, 0, 0:512].rearrange("p (k t) -> p k t", k=2)
        gple = wslot[1][:, 1]

        CH = []
        for c in range(4):
            CH += [(2 * c, "w_gate", c), (2 * c + 1, "w_up", c)]
        CH += [(8 + c, "w_down", c) for c in range(4)]

        @block.sync
        def _(sp):
            for i in range(TI):
                sp.dma_start(h[:, i], a["x"][0, P * i:P * i + P]).then_inc(d_x[i], 16)
                if i == 0:
                    sp.dma_start(cols[:], a["cols"]).then_inc(d_cols, 16)

            def load_win(n):
                sp.dma_start(win[n], a["w_in"][0, :, 512 * GROUPS[n]:512 * GROUPS[n] + 512].rearrange("(k p) n -> p k n", p=P)
                             ).then_inc(d_win[n], 16)

            load_win(0)
            sp.dma_start(zt, a["zt"]).then_inc(d_flt, 16)
            sp.dma_start(wf1, a["flt_w1"][0]).then_inc(d_flt, 16)
            sp.dma_start(wfi, a["flt_w_inner"][0].rearrange("j p n -> p j n")).then_inc(d_flt, 16)
            load_win(1)
            sp.dma_start(rope, a["rope"]).then_inc(d_rope, 16)
            load_win(2)
            sp.dma_start(wfo, a["flt_w_out"][0]).then_inc(d_dec, 16)
            sp.dma_start(decay, a["decay"].rearrange("(i p) n -> p i n", p=P)).then_inc(d_dec, 16)
            load_win(3)
            for n, dst in enumerate((cosf, sinu, sink, sing)):
                sp.dma_start(dst, a["dft"][n].rearrange("(i p) f -> p i f", p=P)).then_inc(d_dft, 16)
            for n in (4, 5):
                load_win(n)
            sp.dma_start(rw[:], a["router_w"][0].rearrange("(k p) n -> p k n", p=P)).then_inc(d_rw, 16)
            sp.dma_start(rb[:], a["router_b"][0:1, :].to_broadcast([P, NE])).then_inc(d_rw, 16)
            for slot, w, c in CH[:8]:
                sp.wait_ge(s["proj"], 2 * (slot // 2) + 2)
                sp.dma_start(wslot[slot], expert_rows(a[w], 0, c)).then_inc(d_w[slot], 16)
            sp.wait_ge(s["proj"], 12)
            sp.dma_start(wout, a["w_out"][0].rearrange("(k p) n -> p k n", p=P)).then_inc(d_wout, 16)
            sp.wait_ge(s["u"], 4)
            sp.dma_start(gffn, a["g_ffn"][0:1, :].to_broadcast([P, D])).then_inc(d_gains, 16)
            sp.wait_ge(s["pr"], 8)
            sp.dma_start(bdn, a["b_down"][0]).then_inc(d_bdn, 16)
            sp.wait_ge(s["yi"], 4)
            for n in range(PARTS):
                rows = bias_in[NE * n:NE * n + NE]
                sp.dma_start(rows[:, 0:D], a["b_gate"][0]).then_inc(d_bias, 16)
                sp.dma_start(rows[:, D:2 * D], a["b_up"][0]).then_inc(d_bias, 16)
            sp.wait_ge(s["mix"], 4)
            for slot, w, c in CH[8:]:
                sp.dma_start(wslot[slot], expert_rows(a[w], 0, c)).then_inc(d_w[slot], 16)
            sp.dma_start(bple, a["b_ple_gate"][0:1, :].to_broadcast([P, D])).then_inc(d_tail, 16)
            sp.dma_start(gfin, a["g_final"].rearrange("(a n) -> a n", a=1).to_broadcast([P, D])).then_inc(d_tail, 16)
            sp.wait_ge(s["tabr"], 3)
            sp.wait_ge(s["tok"], 2)
            sp.wait_ge(s["opened"], 4)
            with sp.Fori(0, NE - 1) as ex:
                before = sp.value_load(table[0:1, bass.ds(ex + TE, 1)], min_val=0, max_val=CHUNKS * NB)
                after = sp.value_load(table[0:1, bass.ds(ex + (TE + 1), 1)], min_val=0, max_val=CHUNKS * NB)
                odd = sp.value_load(table[0:1, bass.ds(ex + (TP + 1), 1)], min_val=0, max_val=1)
                with sp.If(before + 1 <= after):
                    with sp.If(odd >= 1):
                        for slot, w, c in CH[:TWICE]:
                            sp.dma_start(wslot[slot], next_expert_rows(a[w], ex, c)).then_inc(d_w[slot], 16)
                    with sp.If(odd <= 0):
                        for slot, w, c in CH[:TWICE]:
                            sp.dma_start(wother[slot], next_expert_rows(a[w], ex, c)).then_inc(d_wother[slot], 16)
                    for n, (slot, w, c) in enumerate(CH):
                        if n >= TWICE:
                            sp.wait_ge(s["used"], before + (n + 1))
                            sp.dma_start(wslot[slot], next_expert_rows(a[w], ex, c)).then_inc(d_w[slot], 16)
            last = sp.value_load(table[0:1, TE + NE - 1:TE + NE], min_val=0, max_val=CHUNKS * NB)
            sp.wait_ge(s["used"], last + TWICE)
            sp.dma_start(wple, a["w_ple"][0].rearrange("(k p) n -> p k n", p=P)).then_inc(d_ple, 16)
            sp.dma_start(pt, a["pt"].rearrange("(k p) n -> p k n", p=P)).then_inc(d_ple, 16)
            sp.dma_start(gple, a["g_ple"][0:1, :].to_broadcast([P, D])).then_inc(d_gains, 16)
            for n in range(4):
                sp.wait_ge(s["used"], last + (TWICE + n + 1))
                sp.dma_start(wslot[TWICE + n], a["w_ple_gate"][0, 256 * n:256 * n + 256].rearrange("(j p) n -> p j n", p=P)
                             ).then_inc(d_wpg, 16)
            for i in range(TI):
                for hh in range(2):
                    sp.wait_ge(s["fin"], 2 * i + hh + 1)
                    sp.dma_start(out[0, P * i:P * i + P, 512 * hh:512 * hh + 512],
                                 tok[:, i, 512 * hh:512 * hh + 512]).then_inc(s["dout"], 16)
            sp.wait_ge(s["dout"], 2 * 16 * TI)

        @block.gpsimd
        def _(pool):
            pool.wait_ge(s["fd"], 4)
            pool.tensor_tensor(fsum, ffwd, fbwd, ALU.add).then_inc(s["fsum"], 1)
            pool.tensor_tensor(fdif, ffwd, fbwd, ALU.subtract).then_inc(s["fdif"], 1)
            for f in range(TI):
                pool.wait_ge(s["pr"], 4 * f + 4)
                if f == 0:
                    pool.wait_ge(s["ny"], 1)
                pool.tensor_tensor(Yre[:, f], prod[:, 0], prod[:, 1], ALU.subtract).then_inc(s["Y"], 1)
                pool.tensor_tensor(Yim[:, f], prod[:, 2], prod[:, 3], ALU.add).then_inc(s["Y"], 1)
            pool.wait_ge(d_rw, 32)
            pool.tensor_tensor(rw[:], rw[:], col("gffn", 0, KD).rearrange("p (k a) -> p k a", a=1).to_broadcast([P, KD, NE]),
                               ALU.mult).then_inc(s["prep"], 1)
            split = [0]

            def then(ins):
                split[0] += 1
                ins.then_inc(s["split"], 1)
                pool.wait_ge(s["split"], split[0])

            pool.wait_ge(d_bias, 16 * 2 * PARTS)
            for n in (3, 2, 1):
                rows = slice(0, NE * n)
                m = pool.tensor_copy(bias3[rows], bias_in[rows])
                if n > 1:
                    then(m)
                    less = slice(0, NE * (n - 1))
                    then(pool.tensor_tensor(bias_in[less], bias_in[less], bias3[less], ALU.subtract))
                else:
                    m.then_inc(s["prep"], 1)
            pool.wait_ge(s["prep"], 2)
            pool.tensor_copy(ident16, mat("ident")).then_inc(s["prep"], 1)
            for i in range(TI):
                for n in range(2):
                    pool.wait_ge(s["hi"], 2 * i + n + 1)
                    dst = tok[:, i] if n == 0 else tok3[2][:, i]
                    pool.tensor_tensor(dst, tok[:, i], tok3[n][:, i], ALU.subtract).then_inc(s["rest"], 1)

        @block.scalar
        def _(sc):
            def sin_layer(n):
                sc.wait_ge(s["fa"], n + 1)
                sc.activation(fh[:, n], fargs[:, 0], ACT.Sin).then_inc(s["fs"], 1)

            for i in range(TI):
                sc.wait_ge(d_x[i], 16)
                sc.activation(xn[:, i], h[:, i], ACT.Square, accum_out=ssq[:, i:i + 1]).then_inc(s["ssq"], 1)
                sc.wait_ge(s["ssq"], i + 1)
                if i == 0:
                    sc.wait_ge(d_cols, 16)
                sc.activation(std[:, i:i + 1], ssq[:, i:i + 1], ACT.Sqrt, bias=col("eps6"), scale=1.0 / D
                              ).then_inc(s["std"], 1)
            for k in (2, 3, 6, 7):
                sc.wait_ge(s["xT"], k // 2 + 1)
                sc.activation(aT[:, k], half(k // 2, k % 2), ACT.Copy, scale=col("gmix", k)).then_inc(s["aTs"], 1)
            sin_layer(0)
            for n, name in ((0, "rawq"), (1, "rawk")):
                if n:
                    sc.wait_ge(s["rotq"], 1)
                    sc.wait_ge(s["qr"], 1)
                for b in range(2):
                    sc.wait_ge(s["proj"], 2 * n + b + 1)
                    sc.copy(raw[:, 2 * b:2 * b + 2].rearrange("p c t -> p (c t)"), ps[6 + b][:]).then_inc(s[name], 1)
                if n == 0:
                    sin_layer(1)
                    sin_layer(2)
            for i in range(TI):
                sc.wait_ge(s["proj"], 5 + i)
                sc.copy(v[:, i], ps[6 + i][:]).then_inc(s["vv"], 1)
                if i == 0:
                    sc.wait_ge(s["lamp"], 1)
                    sc.activation(lame, ps[5][:, 256:258], ACT.Exp).then_inc(s["lame"], 1)

            def conv_first(n):
                dst = (hv, hx1, hx0)[n // 2]
                sc.wait_ge(s["proj"], 7 + n)
                for c in range(2):
                    ct = 4 * (GROUPS[3 + n // 2] - 3) + 2 * (n % 2) + c
                    sc.activation(dst[:, ct % 4], half(6 + n % 2, c), ACT.Identity, bias=col("cb", ct),
                                  scale=col("cw", 12 + ct)).then_inc(s["projs"], 1)

            def soft(hd):
                sl = hd % 2
                sc.wait_ge(s["nmx"], hd + 1)
                if hd >= 2:
                    sc.wait_ge(s["dT"], hd - 1)
                for c in range(2):
                    for i in range(TI):
                        at = 4 * sl + 2 * c + i
                        sc.activation(E[:, sl, c, i], half(2 * sl + c, i), ACT.Exp, bias=nmx[:, at:at + 1],
                                      scale=SCALE, accum_out=rs[:, at:at + 1]).then_inc(s["ex"], 1)

            def diff_turned(hd):
                sc.wait_ge(s["dT"], hd + 1)
                sc.copy(diffT[:, hd % 2].rearrange("p j q -> p (j q)"), ps[2 * (hd % 2)][:]).then_inc(s["dTs"], 1)

            def head_out(hd):
                sc.wait_ge(s["pv"], hd + 1)
                sc.copy(o[:, hd], half(2 * (hd % 2) + 1, 0)).then_inc(s["o"], 1)

            conv_first(0)
            soft(0)
            conv_first(1)
            soft(1)
            for f in range(TI):
                sc.wait_ge(s["kre"], f + 1)
                sc.activation(Kre[:, f], ps[4 + f][:], ACT.Copy, scale=col("cf", f)).then_inc(s["kres"], 1)
                if f == 0:
                    sc.activation(K0, ps[4][:], ACT.Copy, scale=col("cf", 0)).then_inc(s["kres"], 1)
            conv_first(2)
            diff_turned(0)
            for f in range(TI):
                sc.wait_ge(s["kim"], f + 1)
                sc.activation(Kim[:, f], ps[4 + f][:], ACT.Copy, scale=col("cf", f)).then_inc(s["kims"], 1)
            diff_turned(1)
            head_out(0)
            conv_first(3)
            sc.wait_ge(s["ny"], 1)
            sc.wait_ge(s["kres"], 3)
            sc.activation(K0[0:1, :], ps[4][0:1, :], ACT.Copy, scale=col("cf", 0, 1, 1)).then_inc(s["nys"], 1)
            head_out(1)
            soft(2)
            for i in range(TI):
                sc.wait_ge(s["uT"], i + 1)
                sc.copy(utm[:, i], ps[4 + i][:]).then_inc(s["uts"], 1)
            conv_first(4)
            soft(3)
            conv_first(5)
            diff_turned(2)
            diff_turned(3)
            head_out(2)
            head_out(3)
            sc.wait_ge(s["o"], 4)
            sc.wait_ge(s["dT"], 4)
            sc.activation(sqa, o, ACT.Square).then_inc(s["sqa"], 1)
            for n in range(2):
                sc.wait_ge(s["sna"], n + 1)
                sc.activation(rsa[:, 2 * n:2 * n + 2].rearrange("p c t -> p (c t)"), ps[2 * n][:], ACT.Sqrt,
                              bias=col("eps5"), scale=1.0 / P).then_inc(s["rsa"], 1)
            for c in range(4):
                sc.wait_ge(s["z"], c + 1)
                sc.activation(sqh[:, c], z[:, c], ACT.Square).then_inc(s["sqh"], 1)
            for n in range(2):
                sc.wait_ge(s["snh"], n + 1)
                sc.activation(rsh[:, 2 * n:2 * n + 2].rearrange("p c t -> p (c t)"), ps[4 + n][:], ACT.Sqrt,
                              bias=col("eps6"), scale=1.0 / 64).then_inc(s["rsh"], 1)

            def tok_part(i, n):
                if n == 0:
                    sc.wait_ge(s["tok"], i + 1)
                else:
                    sc.wait_ge(s["rest"], 2 * i + 1)
                sc.copy(tok3[n][:, i], tok[:, i]).then_inc(s["hi"], 1)

            for i in range(TI):
                sc.wait_ge(s["hres"], 2 * i + 2)
                sc.activation(tok3[0][:, i], h[:, i], ACT.Square, accum_out=ssq[:, i:i + 1]).then_inc(s["hsq"], 1)
                sc.wait_ge(s["hsq"], i + 1)
                sc.activation(std[:, i:i + 1], ssq[:, i:i + 1], ACT.Sqrt, bias=col("eps6"), scale=1.0 / D
                              ).then_inc(s["hstd"], 1)
                if i == 0:
                    tok_part(0, 0)

            tok_part(0, 1)
            tok_part(1, 0)
            for i in range(TI):
                sc.wait_ge(s["nm1"], i + 1)
                sc.activation(ew[:, i], lg[:, i], ACT.Exp, bias=nm1[:, i:i + 1]).then_inc(s["ew"], 1)
            tok_part(1, 1)
            sc.wait_ge(s["pwT"], 2)
            sc.copy(pwT[:, 1], ps[5][0:NE, 0:S]).then_inc(s["pwTs"], 1)
            sc.wait_ge(s["tabv"], 1)
            sc.activation(pwT[:, 0], ps[4][0:NE, 0:S], ACT.Identity, bias=first_slot).then_inc(s["pwTs"], 1)
            sc.wait_ge(s["gx"], 1)
            sc.copy(xg, ps[6][:]).then_inc(s["gxs"], 1)
            sc.wait_ge(s["tabr"], 3)
            blocks = sc.value_load(table[0:1, TE + NE - 1:TE + NE], min_val=0, max_val=CHUNKS * NB)
            with sc.Fori(0, NB, LAP) as lap:
                with sc.If(lap * CHUNKS <= blocks):
                    with sc.Fori(lap, lap + LAP) as b:
                        with sc.If(b * CHUNKS <= blocks):
                            sc.wait_ge(s["g"], b + 1)
                            sc.activation(sg, g, ACT.Sigmoid, scale=ALPHA).then_inc(s["sg"], 1)
                            sc.wait_ge(s["sT"], b + 1)
                            sc.copy(selT, ps[4][:, 0:S]).then_inc(s["sTs"], 1)
                            sc.copy(slot_w, ps[4][:, S:S + 1]).then_inc(s["sTs"], 1)
                            sc.wait_ge(s["aTt"], b + 1)
                            sc.copy(actT, ps[5][:]).then_inc(s["aTe"], 1)
                            sc.wait_ge(s["gx"], b + 2)
                            sc.copy(xg, ps[6][:]).then_inc(s["gxs"], 1)
                            sc.wait_ge(s["used"], b * CHUNKS + CHUNKS)
                            sc.wait_ge(s["sTs"], b * 2 + 2)
                            sc.activation(y, ps[7][:], ACT.Copy, scale=slot_w).then_inc(s["yhi"], CHUNKS // 2)
                            sc.wait_ge(s["yhi"], b * CHUNKS + CHUNKS // 2)
                            for hh in range(2):
                                r = slice(64 * hh, 64 * hh + 64)
                                sc.copy(y_big[hh][r, :], y[r, :]).then_inc(s["yhi"], CHUNKS // 4)

            for n in range(4):
                sc.wait_ge(s["eraw"], n + 1)
                sc.copy(e[n // 2][:, 512 * (n % 2):512 * (n % 2) + 512], ps[4 + n][:]).then_inc(s["ers"], 1)
            for i in range(TI):
                sc.wait_ge(s["h2T"], 2 * i + 1)
                sc.copy(hT[:, 0:4, P * i:P * i + P], ps[4 + 2 * i][:].rearrange("p (k t) -> p k t", k=4)
                        ).then_inc(s["h2Ts"], 1)
            sc.wait_ge(s["ers"], 4)
            for i in range(TI):
                sc.activation(squares, e[i], ACT.Square, accum_out=ssq[:, i:i + 1]).then_inc(s["essq"], 1)
                sc.wait_ge(s["essq"], i + 1)
            sc.activation(std, ssq, ACT.Sqrt, bias=col("eps6"), scale=1.0 / D).then_inc(s["estd"], 1)
            for n in range(4):
                i, hh = n // 2, n % 2
                cs = slice(512 * hh, 512 * hh + 512)
                sc.wait_ge(s["gm"], 2 * n + 1)
                sc.activation(tok[:, i, cs], tok[:, i, cs], ACT.Sigmoid).then_inc(s["gsig"], 1)
                sc.wait_ge(s["gm"], 2 * n + 2)
                sc.activation(tok[:, i, cs], h[:, i, cs], ACT.Square, accum_out=fss[:, n:n + 1]).then_inc(s["fsq"], 1)
                if hh:
                    sc.wait_ge(s["fsum2"], i + 1)
                    sc.activation(std[:, i:i + 1], ssq[:, i:i + 1], ACT.Sqrt, bias=col("eps6"), scale=1.0 / D
                                  ).then_inc(s["fstd"], 1)

        @block.tensor
        def _(pe):
            ident, ones = mat("ident"), mat("ones")

            def flt_layer(n):
                if n == 0:
                    pe.wait_ge(d_flt, 48)
                    pe.matmul(ps[5][0:FO, 0:S], wf1, zt, start=True, stop=True).then_inc(s["f1"], 1)
                else:
                    pe.wait_ge(s["fs"], n)
                    pe.matmul(ps[5][0:FO, 0:S], wfi[:, n - 1], fh[:, n - 1], start=True, stop=True
                              ).then_inc(s["f1"], 1)

            def project(n):
                grp, b = n // 2, n % 2
                if b == 0:
                    pe.wait_ge(d_win[grp], 16)
                if n in (2, 3):
                    pe.wait_ge(s["rawq"], b + 1)
                elif n in (4, 5):
                    pe.wait_ge(s["rawk"], b + 1)
                elif n in (6, 7):
                    pe.wait_ge(s["vv"], b + 1)
                elif n >= 8:
                    pe.wait_ge(s["conv"], 2 * (n - 8) + 2)
                if grp == 2:
                    for k in range(KD):
                        m = pe.matmul(ps[6 + b][:], aT[:, k, P * b:P * b + P], win[grp][:, k],
                                      start=k == 0, stop=k == KD - 1)
                else:
                    for c in range(2):
                        for k in range(KD):
                            at = P * (2 * b + c)
                            m = pe.matmul(half(6 + b, c), win[grp][:, k, at:at + P], aT[:, k],
                                          start=k == 0, stop=k == KD - 1)
                m.then_inc(s["proj"], 1)

            def rotate(name, done, b0):
                pe.wait_ge(s[name], 2)
                for c in range(2):
                    m = pe.matmul(ps[b0 + c][:], mat("rot"), raw[:, 2 * c:2 * c + 2].rearrange("p c t -> p (c t)"),
                                  start=True, stop=True)
                m.then_inc(s[done], 1)

            def flt_out(side):
                pe.wait_ge(s["fs"], 3)
                pe.wait_ge(d_dec, 32)
                for i in range(TI):
                    if side:
                        pe.wait_ge(s["fd"], i + 1)
                    pe.matmul(ps[4 + i][:], fh[:, 2, P * i:P * i + P], wfo[:, HW * side:HW * side + HW],
                              start=True, stop=True).then_inc(s["fo"], 1)

            def scores(hd):
                sl = hd % 2
                for i in range(TI):
                    for c in range(2):
                        r = slice(DH * c, DH * c + DH)
                        m = pe.matmul(half(2 * sl + c, i), qrope[r, hd, P * i:P * i + P], krope[r, hd],
                                      start=True, stop=True)
                m.then_inc(s["sc"], 1)

            def turn_diff(hd):
                sl = hd % 2
                pe.wait_ge(s["df"], hd + 1)
                for j in range(TI):
                    for i in range(TI):
                        m = pe.transpose(ps[2 * sl][:, 256 * j + P * i:256 * j + P * i + P],
                                         E[:, sl, 0, i, P * j:P * j + P], ident)
                m.then_inc(s["dT"], 1)

            def apply_v(hd):
                sl = hd % 2
                pe.wait_ge(s["dTs"], hd + 1)
                for j in range(TI):
                    m = pe.matmul(half(2 * sl + 1, 0), v[:, j, P * hd:P * hd + P], diffT[:, sl, j],
                                  start=j == 0, stop=j == 1)
                m.then_inc(s["pv"], 1)

            def spectrum(banks, mat_, data, name):
                for f in range(TI):
                    for i in range(TI):
                        m = pe.matmul(ps[banks[f]][:], mat_[:, i, P * f:P * f + P], data[:, i],
                                      start=i == 0, stop=i == 1)
                    m.then_inc(s[name], 1)

            pe.wait_ge(d_cols, 16)
            for n in range(4):
                for k in (2 * n, 2 * n + 1):
                    for i in range(TI):
                        pe.wait_ge(s["xn"], i + 1)
                        m = pe.transpose(ps[n][:, 256 * (k % 2) + P * i:256 * (k % 2) + P * i + P],
                                         xn[:, i, P * k:P * k + P], ident)
                m.then_inc(s["xT"], 1)
            pe.wait_ge(s["aTv"], 4)
            pe.wait_ge(s["aTs"], 4)
            project(0)
            flt_layer(0)
            project(1)
            flt_layer(1)
            project(2)
            rotate("rawq", "rotq", 0)
            flt_layer(2)
            project(3)
            project(4)
            rotate("rawk", "rotk", 2)
            pe.wait_ge(s["lam"], 1)
            pe.wait_ge(s["fs"], 3)
            pe.matmul(ps[5][:, 256:258], mat("ones", FO), lamp, start=True, stop=True).then_inc(s["lamp"], 1)
            project(5)
            pe.wait_ge(s["lame"], 1)
            flt_out(0)
            project(6)
            pe.wait_ge(s["kr"], 1)
            scores(0)
            flt_out(1)
            project(7)
            scores(1)
            pe.wait_ge(d_dft, 64)
            pe.wait_ge(s["fd"], 4)
            pe.wait_ge(s["fsum"], 1)
            spectrum((4, 5), cosf, fsum, "kre")
            project(8)
            turn_diff(0)
            pe.wait_ge(s["fdif"], 1)
            pe.wait_ge(s["kres"], 3)
            spectrum((4, 5), sink, fdif, "kim")
            apply_v(0)
            turn_diff(1)
            project(9)
            apply_v(1)
            pe.wait_ge(s["kims"], 2)
            for i in range(TI):
                m = pe.matmul(ps[4][0:1, :], sinu[:, i, 0:1], fsum[:, i], start=i == 0, stop=i == 1)
            m.then_inc(s["ny"], 1)
            pe.wait_ge(s["o"], 1)
            scores(2)
            project(10)
            pe.wait_ge(s["u"], 4)
            pe.wait_ge(s["nys"], 1)
            for i in range(TI):
                for c in range(4):
                    m = pe.transpose(ps[4 + i][:, P * c:P * c + P], hv[:, c, P * i:P * i + P], ident)
                m.then_inc(s["uT"], 1)
            pe.wait_ge(s["o"], 2)
            scores(3)
            project(11)
            pe.wait_ge(s["uts"], 2)
            spectrum((4, 5), cosf, utm, "ur")
            pe.wait_ge(s["conv"], 12)
            spectrum((6, 7), sinu, utm, "ui")
            turn_diff(2)
            turn_diff(3)
            apply_v(2)
            apply_v(3)
            pe.wait_ge(s["sqa"], 1)
            for n in range(2):
                pe.matmul(ps[2 * n][:], ones, sqa[:, 2 * n:2 * n + 2].rearrange("p c t -> p (c t)"),
                          start=True, stop=True).then_inc(s["sna"], 1)

            def turn_h(i):
                pe.wait_ge(s["hres"], 2 * i + 2)
                pe.wait_ge(s["z"], 4)
                pe.wait_ge(s["rsh"], 2)
                for n in range(2):
                    for k in range(4):
                        m = pe.transpose(ps[(1, 3, 4, 5)[2 * i + n]][:, P * k:P * k + P],
                                         h[:, i, P * (4 * n + k):P * (4 * n + k) + P], ident)
                    m.then_inc(s["tT"], 1)

            pe.wait_ge(s["Y"], 4)
            for c in range(4):
                terms = [(Yre, cosf, 0), (Yre, cosf, 1), (Yim, sing, 0), (Yim, sing, 1)]
                for n, (yy, w, f) in enumerate(terms):
                    m = pe.matmul(half(1 + 2 * (c // 2), c % 2), yy[:, f, P * c:P * c + P], w[:, f],
                                  start=n == 0, stop=n == 3)
                m.then_inc(s["yi"], 1)

            def hyena_norm(n):
                pe.wait_ge(s["sqh"], 2 * n + 2)
                pe.wait_ge(s["pr"], 8)
                pe.matmul(ps[4 + n][:], mat("blk"), sqh[:, 2 * n:2 * n + 2].rearrange("p c t -> p (c t)"),
                          start=True, stop=True).then_inc(s["snh"], 1)

            def out_proj(n, ks, done=False):
                for k in ks:
                    m = pe.matmul(ps[(0, 2, 6, 7)[n]][:], mixT[:, k, P * (n // 2):P * (n // 2) + P],
                                  wout[:, k, 512 * (n % 2):512 * (n % 2) + 512], start=k == 0, stop=k == KD - 1)
                if done:
                    m.then_inc(s["mix"], 1)

            pe.wait_ge(d_wout, 16)
            pe.wait_ge(s["rsa"], 2)
            pe.wait_ge(s["mixa"], 2)
            out_proj(0, (0, 1))
            out_proj(1, (0, 1))
            hyena_norm(0)
            hyena_norm(1)
            out_proj(2, (0, 1))
            out_proj(3, (0, 1))
            pe.wait_ge(s["mixa"], 4)
            for n in range(4):
                out_proj(n, (2, 3))

            def logits(i):
                pe.wait_ge(s["tTs"], 2 * i + 2)
                for k in range(KD):
                    m = pe.matmul(ps[2 * i][:, 0:NE], tokT[i][:, k], rw[:, k], start=k == 0, stop=k == KD - 1)
                m.then_inc(s["lgt"], 1)

            pe.wait_ge(s["mixh"], 2)
            out_proj(0, (4, 5))
            pe.wait_ge(s["mixh"], 4)
            out_proj(0, (6, 7), True)
            out_proj(1, (4, 5, 6, 7), True)
            out_proj(2, (4, 5, 6, 7), True)
            turn_h(0)
            out_proj(3, (4, 5))
            pe.wait_ge(s["prep"], 1)
            logits(0)
            out_proj(3, (6, 7), True)

            turn_h(1)
            logits(1)
            pe.wait_ge(s["cnt"], 2)
            pe.matmul(ps[6][:, 0:NE], mat("tri"), gt[:, 0], start=True, stop=True)
            pe.matmul(ps[6][:, NE:2 * NE], ones, gt[:, 0], start=True, stop=False)
            pe.matmul(ps[6][:, NE:2 * NE], mat("tri"), gt[:, 1], start=False, stop=True)
            for i in range(TI):
                m = pe.matmul(ps[7][0:NE, 0:1], gt[:, i], ones[:, 0:1], start=i == 0, stop=i == 1)
            m.then_inc(s["pos"], 1)
            pe.wait_ge(s["start"], 1)
            pe.matmul(ps[7][0:NE, 2:4], mat("tri", NE)[:, 0:NE], blocks_used, start=True, stop=True)
            pe.matmul(ps[7][0:1, 64:64 + NE], ne_, mat("tri32i", NE), start=True, stop=True).then_inc(s["tab"], 1)
            pe.wait_ge(s["wr"], 4)
            for i in range(TI):
                pe.transpose(ps[4][0:NE, P * i:P * i + P], ceq[:, i], ident)
                m = pe.transpose(ps[5][0:NE, P * i:P * i + P], ew[:, i], ident)
                m.then_inc(s["pwT"], 1)
            pe.wait_ge(s["tabv"], 2)
            pe.wait_ge(s["pwTs"], 2)
            for i in range(TI):
                pe.matmul(ps[6][:, 64 + NBT * i:64 + NBT * i + NBT], pwT[:, 0, P * i:P * i + P], oh,
                          start=True, stop=True)
                m = pe.matmul(ps[6][:, 192 + NBT * i:192 + NBT * i + NBT], pwT[:, 1, P * i:P * i + P], oh,
                              start=True, stop=True)
            m.then_inc(s["pb"], 1)
            pe.wait_ge(s["load16"], 4)
            for n, what in enumerate((load16, turns16, odd_)):
                pe.matmul(ps[4][0:1, 64 * n:64 * n + NBT], what, oh, start=True, stop=True)
            pe.matmul(ps[4][0:1, 192:192 + NE], odd_, ident[0:NE, 0:NE], start=True, stop=True).then_inc(s["row"], 1)
            for n in range(PARTS):
                m = pe.matmul(ps[4][NE * n:NE * n + NE, 256:256 + NBT], ident[0:NE, 0:NE], oh, start=True, stop=True)
            m.then_inc(s["row"], 1)

            def open_sums(n):
                if n == 0:
                    pe.wait_ge(d_bdn, 16)
                pe.matmul(ps[n][:], pwT[:, 1, P * (n // 2):P * (n // 2) + P], bdn[:, 512 * (n % 2):512 * (n % 2) + 512],
                          start=True, stop=False, skip_group_check=True).then_inc(s["opened"], 1)

            def gather(ks=range(KD)):
                for k in ks:
                    for i in range(TI):
                        for n in range(PARTS):
                            m = pe.matmul(ps[6][:, SLOTS * k:SLOTS * k + SLOTS], tok3[n][:, i, P * k:P * k + P],
                                          sel[:, i], start=i + n == 0, stop=i * n == (TI - 1) * (PARTS - 1))
                if ks[-1] == KD - 1:
                    m.then_inc(s["gx"], 1)

            def scatter(done=None):
                for i in range(TI):
                    for hh in range(2):
                        r = slice(64 * hh, 64 * hh + 64)
                        pe.matmul(ps[2 * i + hh][:], selT[:, P * i:P * i + P], y_big[hh],
                                  start=False, stop=False, skip_group_check=True)
                        m = pe.matmul(ps[2 * i + hh][:], selT[r, P * i:P * i + P], y_last[r, :],
                                      start=False, stop=False, skip_group_check=True)
                    if done is not None:
                        m.then_inc(done, 1)

            pe.wait_ge(s["sel"], 1)
            pe.wait_ge(s["rest"], 4)
            gather()
            for n in range(4):
                open_sums(n)
            pe.wait_ge(s["prep"], 3)

            def gate_up(n, w):
                bk = 4 + n % 2
                for j in range(2):
                    k = 2 * (n // 2) + j
                    for hh in range(2):
                        m = pe.matmul(ps[bk][64 * hh:64 * hh + 64, :], xg[:, SLOTS * k:SLOTS * k + SLOTS],
                                      w[:, j, 512 * hh:512 * hh + 512], start=False, stop=k == KD - 1)
                m.then_inc(s["used"], 1)

            pe.wait_ge(s["tabr"], 3)
            blocks = pe.value_load(table[0:1, TE + NE - 1:TE + NE], min_val=0, max_val=CHUNKS * NB)
            with pe.Fori(0, NB, LAP) as lap:
                with pe.If(lap * CHUNKS <= blocks):
                    with pe.Fori(lap, lap + LAP) as b:
                        with pe.If(b * CHUNKS <= blocks):
                            loaded = pe.value_load(table[0:1, bass.ds(b + TB, 1)], min_val=16, max_val=16 * NE)
                            turns = pe.value_load(table[0:1, bass.ds(b + TT, 1)], min_val=16, max_val=8 * NE)
                            odd = pe.value_load(table[0:1, bass.ds(b + TO, 1)], min_val=0, max_val=1)
                            pe.wait_ge(s["gxs"], b + 1)
                            pe.wait_ge(s["onehot"], b + 1)
                            for bk in (4, 5):
                                for hh in range(2):
                                    at = D * (bk - 4) + 512 * hh
                                    pe.matmul(ps[bk][64 * hh:64 * hh + 64, :], onehot, bias3[:, at:at + 512],
                                              start=True, stop=False)
                            with pe.If(odd >= 1):
                                for n in range(TWICE):
                                    pe.wait_ge(d_w[n], turns)
                                    gate_up(n, wslot[n])
                            with pe.If(odd <= 0):
                                for n in range(TWICE):
                                    pe.wait_ge(d_wother[n], turns)
                                    gate_up(n, wother[n])
                            for n in range(TWICE, 8):
                                pe.wait_ge(d_w[n], loaded)
                                gate_up(n, wslot[n])
                            with pe.If(b >= 1):
                                pe.wait_ge(s["ye"], b * CHUNKS)
                                scatter()
                            pe.wait_ge(s["sel"], b + 2)
                            pe.wait_ge(s["g"], b + 1)
                            for i in range(TI):
                                pe.matmul(ps[4][:, S:S + 1], selw[:, i], ones[:, 0:1], start=i == 0, stop=i == 1)
                            for i in range(TI):
                                m = pe.matmul(ps[4][:, P * i:P * i + P], sel2[:, i], ident16, start=True, stop=True)
                            m.then_inc(s["sT"], 1)
                            gather(range(AHEAD))
                            pe.wait_ge(s["a"], b + 1)
                            for j in range(4):
                                m = pe.transpose(ps[5][:, P * j:P * j + P], act[:, P * j:P * j + P], ident)
                            m.then_inc(s["aTt"], 1)
                            gather(range(AHEAD, KD))
                            pe.wait_ge(s["sTs"], b * 2 + 2)
                            pe.wait_ge(s["aTe"], b + 1)
                            for c in range(4):
                                pe.wait_ge(d_w[8 + c], loaded)
                                for j in range(2):
                                    k = 2 * c + j
                                    at = P * (k % 4) + SLOTS * (k // 4)
                                    for hh in range(2):
                                        m = pe.matmul(ps[7][64 * hh:64 * hh + 64, :], actT[:, at:at + SLOTS],
                                                      wslot[8 + c][:, j, 512 * hh:512 * hh + 512], start=k == 0, stop=k == KD - 1)
                                m.then_inc(s["used"], 1)

            def ple(n):
                for k in range(2):
                    m = pe.matmul(ps[4 + n][:], pt[:, k, P * (n // 2):P * (n // 2) + P],
                                  wple[:, k, 512 * (n % 2):512 * (n % 2) + 512], start=k == 0, stop=k == 1)
                m.then_inc(s["eraw"], 1)

            pe.wait_ge(d_ple, 32)
            ple(0)
            ple(1)
            pe.wait_ge(s["ye"], blocks + CHUNKS)
            scatter(s["scat"])
            ple(2)
            ple(3)

            def turn_h2(i):
                pe.wait_ge(s["h2"], 2 * i + 2)
                pe.wait_ge(s["ers"], 2 * i + 2)
                for n in range(2):
                    for k in range(4):
                        m = pe.transpose(ps[4 + 2 * i + n][:, P * k:P * k + P],
                                         h[:, i, P * (4 * n + k):P * (4 * n + k) + P], ident)
                    m.then_inc(s["h2T"], 1)

            turn_h2(0)
            turn_h2(1)
            pe.wait_ge(d_wpg, 64)
            for n in range(4):
                i, hh = n // 2, n % 2
                if hh == 0:
                    pe.wait_ge(s["h2Ts"], i + 1)
                    pe.wait_ge(s["h2Tv"], i + 1)
                for k in range(KD):
                    m = pe.matmul(ps[n][:], hT[:, k, P * i:P * i + P],
                                  wslot[TWICE + k // 2][:, k % 2, 512 * hh:512 * hh + 512],
                                  start=k == 0, stop=k == KD - 1)
                m.then_inc(s["gate"], 1)

        @block.vector
        def _(dve):
            chain = [0]

            def link(ins):
                chain[0] += 1
                ins.then_inc(s["V"], 1)
                dve.wait_ge(s["V"], chain[0])

            def flt_arg(n):
                dve.wait_ge(s["f1"], n + 1)
                bb = col("b1", 0, 1, FO) if n == 0 else col("binner", n - 1, 1, FO)
                x0, kk = fargs[:, 0], fargs[:, 1]
                if n:
                    dve.wait_ge(s["fs"], n)
                link(dve.tensor_scalar(x0, ps[5][0:FO, 0:S], bb, col("freq", n, 1, FO), ALU.add, ALU.mult))
                link(dve.tensor_scalar(kk, x0, 1.0 / (2 * math.pi), ROUND, ALU.mult, ALU.add))
                link(dve.tensor_scalar(kk, kk, ROUND, None, ALU.subtract))
                for c in TWO_PI:
                    link(dve.scalar_tensor_tensor(x0, kk, -c, x0, ALU.mult, ALU.add))
                dve.tensor_scalar(x0, x0, PI_BELOW, -PI_BELOW, ALU.min, ALU.max).then_inc(s["fa"], 1)

            for i in range(TI):
                dve.wait_ge(s["std"], i + 1)
                link(dve.reciprocal(rstd[:, i:i + 1], std[:, i:i + 1]))
                dve.tensor_scalar(xn[:, i], h[:, i], rstd[:, i:i + 1], None, ALU.mult).then_inc(s["xn"], 1)
            for k in (0, 1, 4, 5):
                dve.wait_ge(s["xT"], k // 2 + 1)
                dve.tensor_scalar(aT[:, k], half(k // 2, k % 2), col("gmix", k), None, ALU.mult).then_inc(s["aTv"], 1)
            flt_arg(0)
            dve.tensor_tensor(lamp, col("lq", 0, 2, FO), col("lk", 0, 2, FO), ALU.mult).then_inc(s["lam"], 1)
            dve.tensor_scalar(subl, col("subln"), 1.0 - LAMBDA_INIT, None, ALU.mult).then_inc(s["lam"], 1)
            flt_arg(1)

            def apply_rope(dst, b0, turned, done):
                dve.wait_ge(s[turned], 1)
                dve.wait_ge(d_rope, 16)
                if dst is qrope:
                    dve.wait_ge(s["xT"], 4)
                for c in range(2):
                    m = dve.tensor_tensor(dst[:, 2 * c:2 * c + 2], ps[b0 + c][:].rearrange("p (c t) -> p c t", c=2),
                                          rope[:, 1:2].to_broadcast([P, 2, S]), ALU.mult)
                link(m)
                link(dve.tensor_tensor(raw, raw, rope[:, 0:1].to_broadcast([P, H, S]), ALU.mult))
                dve.tensor_tensor(dst, dst, raw, ALU.add).then_inc(s[done], 1)

            apply_rope(qrope, 0, "rotq", "qr")
            flt_arg(2)
            apply_rope(krope, 2, "rotk", "kr")

            dve.wait_ge(s["lame"], 1)
            link(dve.tensor_tensor(nlam, lame[:, 1:2], lame[:, 0:1], ALU.subtract))
            link(dve.tensor_scalar(nlam, nlam, LAMBDA_INIT, None, ALU.subtract))

            def decayed(side):
                dst = (ffwd, fbwd)[side]
                for i in range(TI):
                    dve.wait_ge(s["fo"], 2 * side + i + 1)
                    if side == 1:
                        dve.wait_ge(s["fo"], 4)
                    dve.tensor_tensor(dst[:, i], ps[4 + i][:], decay[:, i], ALU.mult).then_inc(s["fd"], 1)

            def conv_rest(n):
                dst = (hv, hx1, hx0)[n // 2]
                dve.wait_ge(s["projs"], 2 * n + 2)
                for c in range(2):
                    ct = 4 * (GROUPS[3 + n // 2] - 3) + 2 * (n % 2) + c
                    x, yy = half(6 + n % 2, c), dst[:, ct % 4]
                    link(dve.scalar_tensor_tensor(yy[:, 1:S], x[:, 0:S - 1], col("cw", ct), yy[:, 1:S],
                                                  ALU.mult, ALU.add))
                    chain[0] += 1
                    dve.scalar_tensor_tensor(yy[:, 0:S - 1], x[:, 1:S], col("cw", 24 + ct), yy[:, 0:S - 1],
                                             ALU.mult, ALU.add).then_inc(s["conv"], 1)
                    chain[0] -= 1

            def maxima(hd):
                sl = hd % 2
                dve.wait_ge(s["sc"], hd + 1)
                for c in range(2):
                    at = 4 * sl + 2 * c
                    m = dve.tensor_reduce(mx[:, at:at + 2], ps[2 * sl + c][:].rearrange("p (i k) -> p i k", i=2),
                                          AX.X, ALU.max)
                link(m)
                dve.tensor_scalar(nmx[:, 4 * sl:4 * sl + 4], mx[:, 4 * sl:4 * sl + 4], -SCALE, None, ALU.mult
                                  ).then_inc(s["nmx"], 1)

            def difference(hd):
                sl = hd % 2
                at = 4 * sl
                dve.wait_ge(s["ex"], 4 * hd + 4)
                link(dve.reciprocal(rsi[:, at:at + 4], rs[:, at:at + 4]))
                link(dve.tensor_scalar(rsi[:, at + 2:at + 4], rsi[:, at + 2:at + 4], nlam, None, ALU.mult))
                for i in range(TI):
                    m = dve.tensor_scalar(E[:, sl, 1, i], E[:, sl, 1, i], rsi[:, at + 2 + i:at + 3 + i], None, ALU.mult)
                link(m)
                for i in range(TI):
                    m = dve.scalar_tensor_tensor(E[:, sl, 0, i], E[:, sl, 0, i], rsi[:, at + i:at + i + 1],
                                                 E[:, sl, 1, i], ALU.mult, ALU.add)
                m.then_inc(s["df"], 1)

            dve.wait_ge(d_dec, 32)
            dve.wait_ge(s["fs"], 3)
            decayed(0)
            conv_rest(0)
            maxima(0)
            decayed(1)
            conv_rest(1)
            difference(0)
            maxima(1)
            conv_rest(2)
            difference(1)
            conv_rest(3)
            dve.wait_ge(s["conv"], 8)
            for c in range(4):
                dve.tensor_tensor(hv[:, c], hv[:, c], hx1[:, c], ALU.mult).then_inc(s["u"], 1)
            maxima(2)
            conv_rest(4)
            difference(2)
            maxima(3)
            conv_rest(5)
            difference(3)
            dve.wait_ge(s["nys"], 1)
            for f in range(TI):
                dve.wait_ge(s["ur"], f + 1)
                dve.wait_ge(s["ui"], f + 1)
                if f:
                    dve.wait_ge(s["Y"], 2)
                ur, ui = ps[4 + f][:], ps[6 + f][:]
                dve.tensor_tensor(prod[:, 0], ur, Kre[:, f], ALU.mult).then_inc(s["pr"], 1)
                dve.tensor_tensor(prod[:, 1], ui, Kim[:, f], ALU.mult).then_inc(s["pr"], 1)
                dve.tensor_tensor(prod[:, 2], ur, Kim[:, f], ALU.mult).then_inc(s["pr"], 1)
                dve.tensor_tensor(prod[:, 3], ui, Kre[:, 1] if f else K0, ALU.mult).then_inc(s["pr"], 1)
            for n in range(2):
                dve.wait_ge(s["rsa"], n + 1)
                link(dve.reciprocal(rsa[:, 2 * n:2 * n + 2], rsa[:, 2 * n:2 * n + 2]))
                if n == 0:
                    dve.wait_ge(s["proj"], 12)
                for hd in (2 * n, 2 * n + 1):
                    dve.scalar_tensor_tensor(mixT[:, hd], o[:, hd], subl, rsa[:, hd], ALU.mult, ALU.mult
                                             ).then_inc(s["mixa"], 1)
            dve.wait_ge(s["uT"], 2)
            for c in range(4):
                dve.wait_ge(s["yi"], 2 * (c // 2) + 2)
                link(dve.scalar_tensor_tensor(z[:, c], hv[:, c], col("dskip", c), half(1 + 2 * (c // 2), c % 2),
                                              ALU.mult, ALU.add))
                dve.tensor_tensor(z[:, c], z[:, c], hx0[:, c], ALU.mult).then_inc(s["z"], 1)
            dve.wait_ge(s["z"], 4)
            for n in range(2):
                dve.wait_ge(s["rsh"], n + 1)
                link(dve.reciprocal(rsh[:, 2 * n:2 * n + 2], rsh[:, 2 * n:2 * n + 2]))
                for c in (2 * n, 2 * n + 1):
                    dve.scalar_tensor_tensor(mixT[:, 4 + c], z[:, c], col("gn", c), rsh[:, c], ALU.mult, ALU.mult
                                             ).then_inc(s["mixh"], 1)
            def token_tile(i):
                dve.scalar_tensor_tensor(tok[:, i], h[:, i], rstd[:, i:i + 1], gffn, ALU.mult, ALU.mult
                                         ).then_inc(s["tok"], 1)

            dve.wait_ge(d_gains, 16)

            def turned(n):
                dve.wait_ge(s["tT"], n + 1)
                dve.tensor_copy(tokT[n // 2][:, 4 * (n % 2):4 * (n % 2) + 4],
                                ps[(1, 3, 4, 5)[n]][:].rearrange("p (k t) -> p k t", k=4)).then_inc(s["tTs"], 1)

            def first_residual(n):
                dve.wait_ge(s["mix"], n + 1)
                hp = h[:, n // 2, 512 * (n % 2):512 * (n % 2) + 512]
                dve.tensor_tensor(hp, ps[(0, 2, 6, 7)[n]][:], hp, ALU.add).then_inc(s["hres"], 1)

            def norm_scale(i):
                dve.wait_ge(s["hstd"], i + 1)
                link(dve.reciprocal(rstd[:, i:i + 1], std[:, i:i + 1]))


            def choose(i):
                dve.wait_ge(s["lgt"], i + 1)
                link(dve.scalar_tensor_tensor(lg[:, i], ps[2 * i][:, 0:NE], rstd[:, i:i + 1], rb[:], ALU.mult, ALU.add))
                link(dve.max(m8[:, i], lg[:, i]))
                dve.tensor_scalar(nm1[:, i:i + 1], m8[:, i, 0:1], -1.0, None, ALU.mult).then_inc(s["nm1"], 1)
                v4 = m8[:, i, TOPK - 1:TOPK]
                dve.tensor_scalar(gt[:, i], lg[:, i], v4, None, ALU.is_gt, ALU.add, accum_out=need[:, i:i + 1])
                link(dve.tensor_scalar(eq[:, i], lg[:, i], v4, None, ALU.is_equal))
                dve.tensor_scalar(need[:, i:i + 1], need[:, i:i + 1], -1.0, float(TOPK), ALU.mult, ALU.add)
                link(dve.tensor_tensor_scan(ceq[:, i], mat("ones")[:, 0:NE], eq[:, i], 0.0, ALU.mult, ALU.add))
                link(dve.scalar_tensor_tensor(eq[:, i], ceq[:, i], need[:, i:i + 1], eq[:, i], ALU.is_le, ALU.mult))
                dve.tensor_tensor(gt[:, i], gt[:, i], eq[:, i], ALU.add).then_inc(s["cnt"], 1)

            first_residual(0)
            first_residual(1)
            norm_scale(0)
            turned(0)
            turned(1)
            token_tile(0)
            first_residual(2)
            choose(0)
            first_residual(3)
            turned(2)
            turned(3)
            norm_scale(1)
            token_tile(1)
            choose(1)
            dve.wait_ge(s["cnt"], 2)
            dve.wait_ge(s["ew"], 2)
            for i in range(TI):
                m = dve.scalar_tensor_tensor(ew[:, i], gt[:, i], 1.0, ew[:, i], ALU.mult, ALU.mult,
                                             accum_out=wsum[:, i:i + 1])
            link(m)
            link(dve.reciprocal(winv, wsum))
            dve.wait_ge(s["pos"], 1)
            cnt = ps[7][0:NE, 0:1]
            link(dve.tensor_scalar(nonempty, cnt, 0.0, col("first", 0, 1, NE), ALU.is_gt, ALU.max))
            link(dve.tensor_scalar(ne_, cnt, float(SLOTS), nonempty, ALU.is_gt, ALU.add))
            link(dve.tensor_scalar(c1, cnt, float(2 * SLOTS), ne_, ALU.is_gt, ALU.add))
            dve.tensor_scalar(ne_, cnt, float(3 * SLOTS), c1, ALU.is_gt, ALU.add).then_inc(s["start"], 1)
            for i in range(TI):
                dve.tensor_scalar(ew[:, i], ew[:, i], winv[:, i:i + 1], None, ALU.mult).then_inc(s["wr"], 1)
                m = dve.scalar_tensor_tensor(ceq[:, i], ps[6][:, NE * i:NE * i + NE], FAR, gt[:, i], ALU.add, ALU.mult)
            link(m)
            for i in range(TI):
                dve.tensor_scalar(ceq[:, i], ceq[:, i], FAR, None, ALU.subtract).then_inc(s["wr"], 1)
            dve.wait_ge(s["tab"], 1)
            link(dve.tensor_copy(starts, ps[7][0:NE, 2:4]))
            dve.tensor_scalar(first_slot, st_, float(SLOTS), None, ALU.mult).then_inc(s["tabv"], 1)
            link(dve.tensor_tensor(en_, st_, ne_, ALU.add))
            link(dve.tensor_scalar(ohs, mat("blkno", NE), st_, None, ALU.is_ge))
            dve.scalar_tensor_tensor(oh, mat("blkno", NE), en_, ohs, ALU.is_lt, ALU.mult).then_inc(s["tabv"], 1)
            dve.tensor_scalar(load16, before_, 16.0, 16.0, ALU.mult, ALU.add).then_inc(s["load16"], 1)
            link(dve.tensor_scalar(pairs_, before_, 0.5, 0.25, ALU.mult, ALU.add))
            link(dve.tensor_scalar(pairs_, pairs_, ROUND, None, ALU.add))
            link(dve.tensor_scalar(pairs_, pairs_, ROUND, None, ALU.subtract))
            dve.scalar_tensor_tensor(odd_, pairs_, -2.0, before_, ALU.mult, ALU.add).then_inc(s["load16"], 1)
            dve.scalar_tensor_tensor(turns16, pairs_, -16.0, load16, ALU.mult, ALU.add).then_inc(s["load16"], 1)
            dve.wait_ge(s["load16"], 3)
            dve.tensor_scalar(odd_, odd_, 1.0, None, ALU.add).then_inc(s["load16"], 1)
            dve.tensor_scalar(table[0:1, TE:TE + NE], ps[7][0:1, 64:64 + NE], float(CHUNKS), -float(CHUNKS),
                              ALU.mult, ALU.add).then_inc(s["tabr"], 1)
            dve.wait_ge(s["pb"], 1)
            for i in range(TI):
                dve.tensor_tensor(posb[:, i], ps[6][:, 64 + NBT * i:64 + NBT * i + NBT], mat("blk64"), ALU.subtract)
                m = dve.tensor_copy(wb[:, i], ps[6][:, 192 + NBT * i:192 + NBT * i + NBT])
            link(m)
            dve.wait_ge(s["prep"], 2)
            for i in range(TI):
                m = dve.tensor_scalar(sel[:, i], mat("slot2")[:, 0:SLOTS], posb[:, i, 0:1], None, ALU.is_equal)
            m.then_inc(s["sel"], 1)
            dve.wait_ge(s["row"], 2)
            dve.tensor_copy(table[0:1, TB:TB + 3 * NBT].rearrange("p (r b) -> p r b", r=3),
                            ps[4][0:1, 0:192].rearrange("p (r b) -> p r b", r=3)[:, :, 0:NBT]).then_inc(s["tabr"], 1)
            dve.tensor_copy(table[0:1, TP:TP + NE], ps[4][0:1, 192:192 + NE]).then_inc(s["tabr"], 1)
            link(dve.tensor_copy(oh3[:, 0:NBT], ps[4][0:PARTS * NE, 256:256 + NBT]))
            dve.tensor_scalar(onehot, mat("ones")[0:PARTS * NE, 0:SLOTS], oh3[:, 0:1], None, ALU.mult
                              ).then_inc(s["onehot"], 1)
            dve.wait_ge(s["tabr"], 3)
            blocks = dve.value_load(table[0:1, TE + NE - 1:TE + NE], min_val=0, max_val=CHUNKS * NB)
            with dve.Fori(0, NB, LAP) as lap:
                with dve.If(lap * CHUNKS <= blocks):
                    with dve.Fori(lap, lap + LAP) as b:
                        with dve.If(b * CHUNKS <= blocks):
                            dve.wait_ge(s["gx"], b + 1)
                            for i in range(TI):
                                dve.tensor_scalar(selw[:, i], mat("slot2"), posb[:, i, bass.ds(b, 1)], wb[:, i, bass.ds(b, 1)],
                                                  ALU.is_equal, ALU.mult)
                                dve.tensor_scalar(sel2[:, i], mat("slot2"), posb[:, i, bass.ds(b, 1)], None, ALU.is_equal)
                            for i in range(TI):
                                m = dve.tensor_scalar(sel[:, i], mat("slot2")[:, 0:SLOTS], posb[:, i, bass.ds(b + 1, 1)], None,
                                                      ALU.is_equal)
                            m.then_inc(s["sel"], 1)
                            dve.wait_ge(s["used"], b * CHUNKS + 8)
                            dve.tensor_scalar(g, ps[4][:], LIMIT, None, ALU.min).then_inc(s["g"], 1)
                            dve.tensor_scalar(u, ps[5][:], LIMIT, -LIMIT, ALU.min, ALU.max).then_inc(s["uc"], 1)
                            dve.wait_ge(s["uc"], b * 2 + 1)
                            dve.scalar_tensor_tensor(u, u, 1.0, g, ALU.add, ALU.mult).then_inc(s["uc"], 1)
                            dve.wait_ge(s["uc"], b * 2 + 2)
                            dve.wait_ge(s["sg"], b + 1)
                            dve.tensor_tensor(act, u, sg, ALU.mult).then_inc(s["a"], 1)
                            dve.tensor_scalar(onehot, mat("ones")[0:PARTS * NE, 0:SLOTS], oh3[:, bass.ds(b + 1, 1)], None,
                                              ALU.mult).then_inc(s["onehot"], 1)
                            dve.wait_ge(s["yhi"], b * CHUNKS + CHUNKS)
                            for hh in range(2):
                                r = slice(64 * hh, 64 * hh + 64)
                                dve.tensor_tensor(y[r, :], y[r, :], y_big[hh][r, :], ALU.subtract
                                                  ).then_inc(s["yr"], CHUNKS // 4)
                            dve.wait_ge(s["yr"], b * CHUNKS + CHUNKS // 2)
                            dve.tensor_copy(y_mid[:], y).then_inc(s["yr"], CHUNKS // 2)
                            dve.wait_ge(s["yr"], b * CHUNKS + CHUNKS)
                            dve.tensor_tensor(y_last, y, y_mid[:], ALU.subtract).then_inc(s["ye"], CHUNKS // 3)
                            for hh in range(2):
                                to, of = slice(64 - 64 * hh, 128 - 64 * hh), slice(64 * hh, 64 * hh + 64)
                                dve.tensor_copy(y_big[hh][to, :], y_mid[of, :]).then_inc(s["ye"], CHUNKS // 3)

            for n in range(4):
                dve.wait_ge(s["scat"], n // 2 + 1)
                hp = h[:, n // 2, 512 * (n % 2):512 * (n % 2) + 512]
                dve.tensor_tensor(hp, ps[n][:], hp, ALU.add).then_inc(s["h2"], 1)
            for i in range(TI):
                dve.wait_ge(s["h2T"], 2 * i + 2)
                dve.tensor_copy(hT[:, 4:8, P * i:P * i + P], ps[5 + 2 * i][:].rearrange("p (k t) -> p k t", k=4)
                                ).then_inc(s["h2Tv"], 1)
            dve.wait_ge(s["estd"], 1)
            link(dve.reciprocal(rstd, std))
            dve.wait_ge(d_gains, 32)
            for i in range(TI):
                dve.scalar_tensor_tensor(e[i], e[i], rstd[:, i:i + 1], gple, ALU.mult, ALU.mult).then_inc(s["en"], 1)
            for n in range(4):
                i, hh = n // 2, n % 2
                cs = slice(512 * hh, 512 * hh + 512)
                dve.wait_ge(s["gate"], n + 1)
                dve.wait_ge(d_tail, 32)
                dve.tensor_tensor(tok[:, i, cs], ps[n][:], bple[:, cs], ALU.add).then_inc(s["gm"], 1)
                dve.wait_ge(s["gsig"], n + 1)
                dve.wait_ge(s["en"], i + 1)
                link(dve.tensor_tensor(e[i][:, cs], tok[:, i, cs], e[i][:, cs], ALU.mult))
                dve.tensor_tensor(h[:, i, cs], h[:, i, cs], e[i][:, cs], ALU.add).then_inc(s["gm"], 1)
                if hh:
                    dve.wait_ge(s["fsq"], n + 1)
                    dve.tensor_tensor(ssq[:, i:i + 1], fss[:, n - 1:n], fss[:, n:n + 1], ALU.add).then_inc(s["fsum2"], 1)
                    dve.wait_ge(s["fstd"], i + 1)
                    link(dve.reciprocal(rstd[:, i:i + 1], std[:, i:i + 1]))
                    dve.wait_ge(d_tail, 32)
                    for c in range(2):
                        cs = slice(512 * c, 512 * c + 512)
                        dve.scalar_tensor_tensor(tok[:, i, cs], h[:, i, cs], rstd[:, i:i + 1], gfin[:, cs],
                                                 ALU.mult, ALU.mult).then_inc(s["fin"], 1)


def shape_constants():
    f32 = np.float32
    t = np.arange(S)
    ang = 2 * np.pi * np.outer(t, t) / NFFT
    cosf = np.cos(ang)
    sink = -np.sin(ang)
    sinu = sink.copy()
    sinu[:, 0] = (-1.0) ** t
    dft = np.stack([cosf, sinu, sink, sinu.T]).astype(f32)
    inv = f32(10000.0) ** (-np.arange(0, DH, 2, dtype=f32) / f32(DH))
    rot_ang = (np.arange(S, dtype=f32)[:, None] * inv[None, :]).astype(f32)
    rope = np.stack([np.tile(np.cos(rot_ang).T, (4, 1)), np.tile(np.sin(rot_ang).T, (4, 1))], 1).astype(f32)
    pos = np.arange(S, dtype=f32)
    tt = (pos / f32(S - 1)).astype(f32)
    bands = (EMB - 1) // 2
    f = np.linspace(1e-4, bands - 1, bands, dtype=f32)
    fw = (((f32(2.0 * math.pi / S)) * pos)[:, None] * f[None, :]).astype(f32)
    zt = np.concatenate([tt[:, None], np.cos(fw), -np.sin(fw)], axis=-1).astype(f32).T
    lo, hi = math.log(1e-2) / 1.5, math.log(1e-2) / 0.3
    deltas = np.abs(np.linspace(lo, hi, HW, dtype=f32))
    decay = np.exp(-tt[:, None] * deltas[None, :]).astype(f32)
    c = {}
    c["cf"] = np.full((P, TI), 2.0 / NFFT)
    c["cf"][0, 0] = 1.0 / NFFT
    c["eps6"] = np.full((P, 1), 1e-6)
    c["eps5"] = np.full((P, 1), 1e-5)
    c["first"] = np.arange(P)[:, None] == 0
    c["ident"] = np.eye(P)
    r = np.zeros((P, P))
    for m in range(P):
        if m % 64 < 32:
            r[m + 32, m] = -1.0
        else:
            r[m - 32, m] = 1.0
    c["rot"] = r
    c["blk"] = np.kron(np.eye(2), np.ones((64, 64)))
    c["tri"] = np.triu(np.ones((P, P)), 1)
    c["ones"] = np.ones((P, P))
    c["slot2"] = np.tile(np.arange(SLOTS), (P, 2))
    c["blkno"] = np.tile(np.arange(NBT), (P, 1))
    c["blk64"] = SLOTS * c["blkno"]
    c["tri32i"] = np.triu(np.ones((P, NE)))
    return dft, rope, zt, decay, {k: np.asarray(v_, f32) for k, v_ in c.items()}


def kernel(**inputs):
    import concourse.bacc as bacc
    from concourse.bass_utils import run_bass_kernel_spmd as run

    dft, rope, zt, decay, c = shape_constants()
    given = {k: np.asarray(v_) for k, v_ in inputs.items()}

    def per_partition(vec, n):
        return vec.reshape(n, P).T

    def on_64(rows):
        return np.concatenate([rows.T, rows.T], axis=0)

    c["gmix"] = per_partition(given["g_mix"][0], KD)
    c["gffn"] = per_partition(given["g_ffn"][0], KD)
    c["cw"] = np.concatenate([per_partition(given["hyena_conv_w"][0, j], 12) for j in range(3)], axis=1)
    c["cb"] = per_partition(given["hyena_conv_b"][0], 12)
    c["dskip"] = per_partition(given["hyena_d"][0], 4)
    c["gn"] = per_partition(given["hyena_gn"][0], 4)
    c["subln"] = given["attn_subln"][0].reshape(P, 1)
    c["b1"] = on_64(given["flt_b1"])
    c["binner"] = on_64(given["flt_b_inner"][0])
    c["freq"] = on_64(given["flt_freq"][0])
    c["lq"] = on_64(np.concatenate([given["lambda_q1"], given["lambda_q2"]], axis=0))
    c["lk"] = on_64(np.concatenate([given["lambda_k1"], given["lambda_k2"]], axis=0))
    arrays = {
        "cols": np.concatenate([c[n] for n in COLS], axis=1),
        "rope": rope, "dft": dft, "decay": decay, "zt": zt,
        "pt": given["p"][0, 0].T,
    }
    nc = bacc.Bacc("TRN2", target_bir_lowering=False, num_devices=1)
    feeds, aps = {}, {}
    for name in INPUTS:
        arr = np.ascontiguousarray(arrays[name] if name in arrays else given[name])
        feeds["in_" + name] = arr
        aps[name] = nc.dram_tensor("in_" + name, arr.shape, mybir.dt.from_np(arr.dtype), kind="ExternalInput").ap()
    out = nc.dram_tensor("out", (1, S, D), F32, kind="ExternalOutput").ap()
    build(nc, aps, out)
    r = run(nc, [feeds], core_ids=[0])
    return r.results[0]["out"]
```
